# Optimizing a Trainium2 kernel written in Bass

```python
import jax
import jax.numpy as jnp
from jax import lax
import numpy as np

D_MODEL = 1024
BATCH = 1
SEQ = 128
DEPTH = 2
DEC_BATCH = 1
DEC_SEQ = 512
PAST_LEN = 128

GRID_W = 64
EPS = 1e-6
N_EVEN = (DEPTH + 1) // 2
N_ODD = DEPTH // 2
D_CONV = D_MODEL // 2
HG_HEADS = 4
HG_DK = 128
HG_DV = 128
HG_WK = HG_HEADS * HG_DK
HG_WV = HG_HEADS * HG_DV
HG_CHUNK = 16
EVEN_IN = 3 * D_CONV + 3 * HG_WK + 2 * HG_WV
EVEN_MIX = D_CONV + HG_WV
HEAD_DIM = 64
ATT_HEADS = 8
ATT_KV = 2
ATT_GROUP = ATT_HEADS // ATT_KV
ATT_QW = ATT_HEADS * HEAD_DIM
ATT_KVW = ATT_KV * HEAD_DIM
ODD_IN = 2 * (ATT_QW + 2 * ATT_KVW)
ODD_MIX = 2 * ATT_QW
Q_BLOCK = 128
WINDOW = 128
ROPE_THETA = 10000.0
ROPE_AXIS = HEAD_DIM // 2
ROPE_FREQS = ROPE_AXIS // 2
PEER_HEADS = 8
PEER_DQ = 256
PEER_HALF = PEER_DQ // 2
N_KEYS = 128
N_EXPERTS = N_KEYS * N_KEYS
PEER_TOPK = 16
PEER_TBLK = 128

kernel_name = "hybrid_diffusion_prefix_step"

def rmsnorm(x, g):
    xf = x.astype(jnp.float32)
    y = xf * lax.rsqrt(jnp.mean(xf * xf, axis=-1, keepdims=True) + EPS)
    return (y * g.astype(jnp.float32)).astype(x.dtype)

def modulate(x, g, shift, scale):
    return rmsnorm(x, g) * (1.0 + scale) + shift

def adaln(cvec, w, b):
    return jnp.split(jax.nn.silu(cvec) @ w + b, 6, axis=-1)

def _split(p, sizes):
    idx = [int(i) for i in np.cumsum(sizes)[:-1]]
    return jnp.split(p, idx, axis=-1)

def grid_rope_tables(rows, dtype):
    row = jnp.repeat(jnp.arange(rows, dtype=jnp.float32), GRID_W)
    col = jnp.tile(jnp.arange(GRID_W, dtype=jnp.float32), rows)
    inv = ROPE_THETA ** (-jnp.arange(ROPE_FREQS, dtype=jnp.float32) / ROPE_FREQS)
    ang = jnp.concatenate([row[:, None] * inv[None], col[:, None] * inv[None]], axis=-1)
    return jnp.cos(ang).astype(dtype), jnp.sin(ang).astype(dtype)

def apply_rope(x, cos, sin):
    shp = (1, x.shape[1]) + (1,) * (x.ndim - 3) + (ROPE_FREQS,)
    out = []
    for a in range(2):
        xa = x[..., a * ROPE_AXIS:(a + 1) * ROPE_AXIS]
        x1, x2 = xa[..., :ROPE_FREQS], xa[..., ROPE_FREQS:]
        c = cos[:, a * ROPE_FREQS:(a + 1) * ROPE_FREQS].reshape(shp)
        s = sin[:, a * ROPE_FREQS:(a + 1) * ROPE_FREQS].reshape(shp)
        out += [x1 * c - x2 * s, x1 * s + x2 * c]
    return jnp.concatenate(out, axis=-1)

def short_conv(u, w):
    up = jnp.pad(u, ((0, 0), (1, 1), (0, 0)))
    return up[:, :-2] * w[0] + up[:, 1:-1] * w[1] + up[:, 2:] * w[2]

def hgrn_chunked(q, k, v, logf, s0):
    B, L, H, K = q.shape
    V = v.shape[-1]
    n = L // HG_CHUNK
    f32 = jnp.float32
    rs = lambda a: a.astype(f32).reshape(B, n, HG_CHUNK, H, a.shape[-1])
    q, k, v, logf = rs(q), rs(k), rs(v), rs(logf)
    b = jnp.cumsum(logf, axis=2)
    mask = jnp.tril(jnp.ones((HG_CHUNK, HG_CHUNK), bool))[None, None, :, :, None, None]
    diff = b[:, :, :, None] - b[:, :, None, :]
    decay = jnp.exp(jnp.where(mask, diff, -jnp.inf))
    attn = jnp.einsum('bnthk,bnshk,bntshk->bnhts', q, k, decay)
    o_intra = jnp.einsum('bnhts,bnshv->bnthv', attn, v)
    b_last = b[:, :, -1]
    k_dec = k * jnp.exp(b_last[:, :, None] - b)
    d_state = jnp.einsum('bnshk,bnshv->bnhkv', k_dec, v)

    def step(S, inp):
        g, d = inp
        return S * g[..., None] + d, S

    s_fin, s_prev = lax.scan(step, s0.astype(f32),
                             (jnp.moveaxis(jnp.exp(b_last), 1, 0), jnp.moveaxis(d_state, 1, 0)))
    o_inter = jnp.einsum('bnthk,nbhkv->bnthv', q * jnp.exp(b), s_prev)
    return (o_intra + o_inter).reshape(B, L, H, V), s_fin

def even_mix(h, w_in, conv_w, w_out, lb, onorm_g, s0):
    B, L, _ = h.shape
    gb, gc, u, q, zf, zb, iv, og = _split(h @ w_in, [D_CONV] * 3 + [HG_WK] * 3 + [HG_WV] * 2)
    a_out = gb * short_conv(gc * u, conv_w)
    q = jax.nn.silu(q).reshape(B, L, HG_HEADS, HG_DK)
    v = iv.reshape(B, L, HG_HEADS, HG_DV)
    outs, finals = [], []
    for d, z in enumerate((zf, zb)):
        zf32 = z.astype(jnp.float32)
        lbd = lb[d]
        logf = jnp.log(lbd + (1.0 - lbd) * jax.nn.sigmoid(zf32)).reshape(B, L, HG_HEADS, HG_DK)
        kk = ((1.0 - lbd) * jax.nn.sigmoid(-zf32)).reshape(B, L, HG_HEADS, HG_DK)
        if d == 0:
            o, sf = hgrn_chunked(q, kk, v, logf, s0[:, 0])
        else:
            o, sf = hgrn_chunked(jnp.flip(q, 1), jnp.flip(kk, 1), jnp.flip(v, 1), jnp.flip(logf, 1), s0[:, 1])
            o = jnp.flip(o, 1)
        outs.append(o)
        finals.append(sf)
    o = (outs[0] + outs[1]).astype(h.dtype)
    o = rmsnorm(o, onorm_g.reshape(HG_HEADS, HG_DV)) * jax.nn.silu(og).reshape(B, L, HG_HEADS, HG_DV)
    y = jnp.concatenate([a_out, o.reshape(B, L, HG_WV)], axis=-1) @ w_out
    return y, jnp.stack(finals, axis=1).astype(h.dtype)

def odd_project(h, w_in, qn_g, kn_g):
    B, L, _ = h.shape
    qc, kc, vc, qd, kd, vd = _split(h @ w_in, [ATT_QW, ATT_KVW, ATT_KVW] * 2)
    qs = (B, L, ATT_KV, ATT_GROUP, HEAD_DIM)
    ks = (B, L, ATT_KV, HEAD_DIM)
    qc = rmsnorm(qc.reshape(qs), qn_g)
    kc = rmsnorm(kc.reshape(ks), kn_g)
    return qc, kc, vc.reshape(ks), qd.reshape(qs), kd.reshape(ks), vd.reshape(ks)

def odd_out(oc, od, w_out):
    B, L = oc.shape[:2]
    return jnp.concatenate([oc.reshape(B, L, ATT_QW), od.reshape(B, L, ATT_QW)], axis=-1) @ w_out

def block_attn(q, k, v, sink):
    B, Lq = q.shape[:2]
    nb = Lq // Q_BLOCK
    qb = jnp.moveaxis(q.reshape((B, nb, Q_BLOCK) + q.shape[2:]), 1, 0)
    scale = HEAD_DIM ** -0.5

    def one(qi):
        s = jnp.einsum('bqhgd,bshd->bhgqs', qi, k).astype(jnp.float32) * scale
        if sink is None:
            p = jax.nn.softmax(s, axis=-1)
        else:
            sk = jnp.broadcast_to(sink.astype(jnp.float32).reshape(1, ATT_KV, ATT_GROUP, 1, 1), s.shape[:-1] + (1,))
            p = jax.nn.softmax(jnp.concatenate([s, sk], axis=-1), axis=-1)[..., :-1]
        return jnp.einsum('bhgqs,bshd->bqhgd', p.astype(v.dtype), v)

    o = lax.map(one, qb)
    return jnp.moveaxis(o, 0, 1).reshape(q.shape)

def window_attn(q, k, v, k_ctx, v_ctx, sink):
    B, L = q.shape[:2]
    Lc = k_ctx.shape[1]
    nb = L // Q_BLOCK
    span = Q_BLOCK + 2 * WINDOW
    pad = ((0, 0), (WINDOW, WINDOW), (0, 0), (0, 0))
    idx = jnp.arange(nb)[:, None] * Q_BLOCK + jnp.arange(span)[None, :]
    kb = jnp.pad(k, pad)[:, idx]
    vb = jnp.pad(v, pad)[:, idx]
    qb = q.reshape(B, nb, Q_BLOCK, ATT_KV, ATT_GROUP, HEAD_DIM)
    scale = HEAD_DIM ** -0.5
    s_loc = jnp.einsum('bnqhgd,bnshd->bnhgqs', qb, kb).astype(jnp.float32) * scale
    s_ctx = jnp.einsum('bnqhgd,bchd->bnhgqc', qb, k_ctx).astype(jnp.float32) * scale
    qpos = jnp.arange(nb)[:, None] * Q_BLOCK + jnp.arange(Q_BLOCK)[None, :]
    kpos = idx - WINDOW
    rel = kpos[:, None, :] - qpos[:, :, None]
    valid = (jnp.abs(rel) <= WINDOW) & (kpos[:, None, :] >= 0) & (kpos[:, None, :] < L)
    s_loc = jnp.where(valid[None, :, None, None], s_loc, -jnp.inf)
    sk = jnp.broadcast_to(sink.astype(jnp.float32).reshape(1, 1, ATT_KV, ATT_GROUP, 1, 1), s_loc.shape[:-1] + (1,))
    p = jax.nn.softmax(jnp.concatenate([s_loc, s_ctx, sk], axis=-1), axis=-1).astype(v.dtype)
    o = (jnp.einsum('bnhgqs,bnshd->bnqhgd', p[..., :span], vb)
         + jnp.einsum('bnhgqc,bchd->bnqhgd', p[..., span:span + Lc], v_ctx))
    return o.reshape(q.shape)

def peer(h, w_q, subkeys, u_tab, v_tab):
    B, L, D = h.shape
    T = B * L
    ht = h.reshape(T, D)
    q = (ht @ w_q).reshape(T, PEER_HEADS, 2, PEER_HALF)
    s = jnp.einsum('thpd,hpnd->thpn', q, subkeys).astype(jnp.float32)
    s1, i1 = lax.top_k(s[:, :, 0], PEER_TOPK)
    s2, i2 = lax.top_k(s[:, :, 1], PEER_TOPK)
    cand = (s1[..., :, None] + s2[..., None, :]).reshape(T, PEER_HEADS, PEER_TOPK * PEER_TOPK)
    cidx = (i1[..., :, None] * N_KEYS + i2[..., None, :]).reshape(T, PEER_HEADS, PEER_TOPK * PEER_TOPK)
    sc, pos = lax.top_k(cand, PEER_TOPK)
    eidx = jnp.take_along_axis(cidx, pos, axis=-1)
    gate = jax.nn.softmax(sc, axis=-1).astype(h.dtype)
    nt = T // PEER_TBLK
    xb = ht.reshape(nt, PEER_TBLK, D)
    eb = eidx.reshape(nt, PEER_TBLK, PEER_HEADS * PEER_TOPK)
    gb = gate.reshape(nt, PEER_TBLK, PEER_HEADS * PEER_TOPK)

    def expert_block(args):
        xi, ei, gi = args
        a = jax.nn.gelu(jnp.einsum('td,tkd->tk', xi, u_tab[ei]), approximate=False)
        return jnp.einsum('tk,tkd->td', gi * a, v_tab[ei])

    y = lax.map(expert_block, (xb, eb, gb))
    return y.reshape(B, L, D)

def setup_inputs(seed: int = 0) -> dict:
    key = jax.random.key(seed)
    ks = jax.random.split(key, 28)
    n = lambda i, shape, s: jax.random.normal(ks[i], shape, jnp.float32) * s
    kv_shape = (DEC_BATCH, N_ODD, PAST_LEN, ATT_KV, HEAD_DIM)
    return {
        "x_prompt": n(0, (BATCH, SEQ, D_MODEL), 1.0),
        "x_sample": n(1, (DEC_BATCH, DEC_SEQ, D_MODEL), 1.0),
        "c": n(2, (DEC_BATCH, D_MODEL), 1.0),
        "c_ctx": n(3, (D_MODEL,), 1.0),
        "state_hgrn": n(4, (DEC_BATCH, N_EVEN, 2, HG_HEADS, HG_DK, HG_DV), 0.5),
        "cache_c_k": n(5, kv_shape, 1.0),
        "cache_c_v": n(6, kv_shape, 1.0),
        "cache_d_k": n(7, kv_shape, 1.0),
        "cache_d_v": n(8, kv_shape, 1.0),
        "norm1_g": 1.0 + n(9, (DEPTH, D_MODEL), 0.01),
        "norm2_g": 1.0 + n(10, (DEPTH, D_MODEL), 0.01),
        "w_mod": n(11, (DEPTH, D_MODEL, 6 * D_MODEL), 0.5 * D_MODEL ** -0.5),
        "b_mod": n(12, (DEPTH, 6 * D_MODEL), 0.01),
        "even_w_in": n(13, (N_EVEN, D_MODEL, EVEN_IN), D_MODEL ** -0.5),
        "even_conv_w": n(14, (N_EVEN, 3, D_CONV), 0.5),
        "even_w_out": n(15, (N_EVEN, EVEN_MIX, D_MODEL), EVEN_MIX ** -0.5),
        "lb_logits": n(16, (DEPTH + 1, 2, HG_WK), 0.5),
        "hgrn_onorm_g": 1.0 + n(17, (N_EVEN, HG_WV), 0.01),
        "odd_w_in": n(18, (N_ODD, D_MODEL, ODD_IN), D_MODEL ** -0.5),
        "attn_qnorm_g": 1.0 + n(19, (N_ODD, HEAD_DIM), 0.01),
        "attn_knorm_g": 1.0 + n(20, (N_ODD, HEAD_DIM), 0.01),
        "attn_sink": n(21, (N_ODD, ATT_HEADS), 0.5),
        "odd_w_out": n(22, (N_ODD, ODD_MIX, D_MODEL), ODD_MIX ** -0.5),
        "peer_w_q": n(23, (DEPTH, D_MODEL, PEER_HEADS * PEER_DQ), D_MODEL ** -0.5),
        "peer_subkeys": n(24, (DEPTH, PEER_HEADS, 2, N_KEYS, PEER_HALF), PEER_HALF ** -0.5),
        "peer_u": n(25, (DEPTH, N_EXPERTS, D_MODEL), D_MODEL ** -0.5),
        "peer_v": n(26, (DEPTH, N_EXPERTS, D_MODEL), PEER_HEADS ** -0.5),
        "final_g": 1.0 + n(27, (D_MODEL,), 0.01),
    }

def reference(x_prompt, x_sample, c, c_ctx, state_hgrn, cache_c_k, cache_c_v, cache_d_k, cache_d_v,
              norm1_g, norm2_g, w_mod, b_mod, even_w_in, even_conv_w, even_w_out, lb_logits, hgrn_onorm_g,
              odd_w_in, attn_qnorm_g, attn_knorm_g, attn_sink, odd_w_out,
              peer_w_q, peer_subkeys, peer_u, peer_v, final_g):
    lb_all = jnp.cumsum(jax.nn.softmax(lb_logits.astype(jnp.float32), axis=0), axis=0)
    rows = x_sample.shape[1] // GRID_W
    cos, sin = grid_rope_tables(rows, x_sample.dtype)
    xc, xs = x_prompt, x_sample
    Bc = xc.shape[0]
    new_hgrn, new_ck, new_cv, new_dk, new_dv = [], [], [], [], []
    for l in range(DEPTH):
        j = l // 2
        sh1c, sc1c, g1c, sh2c, sc2c, g2c = adaln(c_ctx[None, None, :], w_mod[l], b_mod[l])
        sh1s, sc1s, g1s, sh2s, sc2s, g2s = adaln(c[:, None, :], w_mod[l], b_mod[l])
        hc = modulate(xc, norm1_g[l], sh1c, sc1c)
        hs = modulate(xs, norm1_g[l], sh1s, sc1s)
        if l % 2 == 0:
            zeros0 = jnp.zeros((Bc, 2, HG_HEADS, HG_DK, HG_DV), xc.dtype)
            yc, st = even_mix(hc, even_w_in[j], even_conv_w[j], even_w_out[j], lb_all[l], hgrn_onorm_g[j], zeros0)
            ys, _ = even_mix(hs, even_w_in[j], even_conv_w[j], even_w_out[j], lb_all[l], hgrn_onorm_g[j],
                             state_hgrn[:, j])
            new_hgrn.append(st)
        else:
            qc, kc, vc, qd, kd, vd = odd_project(hc, odd_w_in[j], attn_qnorm_g[j], attn_knorm_g[j])
            yc = odd_out(block_attn(qc, kc, vc, None), block_attn(qd, kd, vd, attn_sink[j]), odd_w_out[j])
            new_ck.append(kc)
            new_cv.append(vc)
            new_dk.append(kd)
            new_dv.append(vd)
            qc, kc, vc, qd, kd, vd = odd_project(hs, odd_w_in[j], attn_qnorm_g[j], attn_knorm_g[j])
            qc, kc = apply_rope(qc, cos, sin), apply_rope(kc, cos, sin)
            qd, kd = apply_rope(qd, cos, sin), apply_rope(kd, cos, sin)
            oc = block_attn(qc, jnp.concatenate([cache_c_k[:, j], kc], axis=1),
                            jnp.concatenate([cache_c_v[:, j], vc], axis=1), None)
            od = window_attn(qd, kd, vd, cache_d_k[:, j], cache_d_v[:, j], attn_sink[j])
            ys = odd_out(oc, od, odd_w_out[j])
        xc = xc + g1c * yc
        xs = xs + g1s * ys
        hc = modulate(xc, norm2_g[l], sh2c, sc2c)
        hs = modulate(xs, norm2_g[l], sh2s, sc2s)
        xc = xc + g2c * peer(hc, peer_w_q[l], peer_subkeys[l], peer_u[l], peer_v[l])
        xs = xs + g2s * peer(hs, peer_w_q[l], peer_subkeys[l], peer_u[l], peer_v[l])
    y_prompt = rmsnorm(xc, final_g)
    y_sample = rmsnorm(xs, final_g)
    return (y_prompt, y_sample, jnp.stack(new_hgrn, axis=1), jnp.stack(new_ck, axis=1), jnp.stack(new_cv, axis=1),
            jnp.stack(new_dk, axis=1), jnp.stack(new_dv, axis=1))


_drawn_inputs = setup_inputs


def setup_inputs(seed=0):
    import zlib

    import numpy as np

    out = dict(_drawn_inputs(seed))
    spreads = {}
    factors = {'state_hgrn': 200.0,
     'cache_c_k': 8.0,
     'cache_c_v': 6.925,
     'cache_d_k': 127.192,
     'cache_d_v': 152.144,
     'norm1_g': 13.865,
     'norm2_g': 200.0,
     'b_mod': 2.928,
     'hgrn_onorm_g': 200.0,
     'attn_qnorm_g': 200.0,
     'attn_knorm_g': 200.0,
     'attn_sink': 8.0,
     'final_g': 200.0,
     'odd_w_out': 6.731}
    for name, (base, spread) in spreads.items():
        noise = np.random.default_rng([zlib.crc32(name.encode()), seed]).standard_normal(out[name].shape)
        drawn = base * np.exp(spread * noise) if base else spread * noise
        out[name] = jnp.asarray(drawn.astype(out[name].dtype))
    for name, factor in factors.items():
        out[name] = (out[name] * factor).astype(out[name].dtype)
    return out
```

```python
from contextlib import ExitStack, contextmanager

import concourse.bass as bass
from concourse import mybir

F32 = mybir.dt.float32
U32 = mybir.dt.uint32
ALU = mybir.AluOpType
ACT = mybir.ActivationFunctionType
AX = mybir.AxisListType

P = 128
LOWEST = -3.0e38


class Chain:

    def __init__(self, engine, sem, offset=0, step=None):
        self.engine, self.sem, self.n, self.offset, self.step = engine, sem, 0, offset, step

    def __call__(self, instruction):
        instruction.then_inc(self.sem, 1)
        self.n += 1
        hold(self.engine, self.sem, self.offset + self.n, self.step)


class Shapes:
    def __init__(self, x_prompt, x_sample, even_w_in, lb_logits, odd_w_in, peer_w_q, peer_subkeys, cache_c_k):
        self.D = x_prompt.shape[2]
        self.KD = self.D // P
        self.SC, self.SS = x_prompt.shape[1], x_sample.shape[1]
        assert self.SC == P and self.SS % P == 0
        self.TS = self.SS // P
        self.T = 1 + self.TS
        self.N = self.T * P
        self.DEPTH = peer_w_q.shape[0]
        self.W2 = self.D // 2
        self.H = self.W2 // P
        self.HEADS, self.E = peer_subkeys.shape[1], peer_subkeys.shape[3]
        self.PAST = cache_c_k.shape[2]


@contextmanager
def phase(nc, names):
    with ExitStack() as stack:
        sems = {}
        for name in names.split():
            name, _, n = name.partition("*")
            if n:
                sems[name] = [stack.enter_context(nc.semaphore(f"{name}{i}")) for i in range(int(n))]
            else:
                sems[name] = stack.enter_context(nc.semaphore(name))
        with nc.Block() as block:
            yield block, type("Semaphores", (), sems)
        flat = [s for v in sems.values() for s in (v if isinstance(v, list) else [v])]
        for s in flat:
            nc.gpsimd.sem_clear(s)
        nc.all_engine_barrier()


class Memory:
    pass


class Early:

    def __init__(self, sems):
        self.sems, self.n = sems, [0] * len(sems)

    def load(self, sp, i, dst, src):
        self.n[i] += 1
        sp.dma_start(dst, src).then_inc(self.sems[i], 16)

    def wait(self, engine, i):
        engine.wait_ge(self.sems[i], 16 * self.n[i])


def columns(w, n):
    return w[:, n * 512:(n + 1) * 512].rearrange("(k p) n -> p k n", p=P)


def two_slots(m, s, at):
    return [m.arena[:, o:o + s.KD * 512].rearrange("p (k n) -> p k n", n=512) for o in at]


def build(nc, a, out, stop=None, dump=None):
    s = Shapes(a.x_prompt, a.x_sample, a.even_w_in, a.lb_logits, a.odd_w_in, a.peer_w_q, a.peer_subkeys,
               a.cache_c_k)
    D, KD, T, N = s.D, s.KD, s.T, s.N
    with ExitStack() as ctx:
        def sb(name, shape, dt=F32):
            return ctx.enter_context(nc.sbuf_tensor(name, shape, dt))

        m = Memory()
        m.x = sb("x", [P, T, D])
        m.h = sb("h", [P, T, D])
        m.hT = sb("hT", [P, KD, N])
        m.shift = sb("mod_shift", [P, 2, D])
        m.scale = sb("mod_scale", [P, 2, D])
        m.gate = sb("mod_gate", [P, 2, D])
        m.ident = sb("ident", [P, P])
        m.cT = sb("silu_c", [P, KD, 2])
        m.pick = sb("pick_row", [2, 2, P])
        m.eps = sb("eps", [P, 1])
        m.ones = sb("ones", [P, P])
        m.small = sb("small", [P, 256])
        m.iota = sb("iota", [P, 16])[:]
        m.tail = sb("tail", [P, 96])
        m.arena = sb("arena", [P, ARENA])
        m.mod_rows = nc.dram_tensor("mod_rows", [2 * s.DEPTH, 2, 3 * D], F32).ap()
        m.ps = ctx.enter_context(nc.psum_tensor("ps", [P, 8, 512], F32))
        m.u_landed, m.v_landed = ([ctx.enter_context(nc.semaphore(f"{name}{i}")) for i in range(SLOTS)]
                                  for name in ("u_landed", "v_landed"))
        m.rows_stored, m.stores = ctx.enter_context(nc.semaphore("rows_stored")), 0
        m.early = Early([ctx.enter_context(nc.semaphore(f"early_landed{i}")) for i in range(3)])

        stages = [("setup", lambda: setup(nc, s, m, a))]
        for l in range(s.DEPTH):
            even, j = l % 2 == 0, l // 2
            w_in = (a.even_w_in if even else a.odd_w_in)[j]
            w_out = (a.even_w_out if even else a.odd_w_out)[j]
            first = modulation if l == 0 else modulate
            to_project = first_weights(m, (even_slots if even else odd_slots)(s, m), w_in)
            out_slots = mix_slots(s, m, even)[0]
            stages.append((f"mod{l}0", lambda l=l, f=first, e=to_project: f(nc, s, m, a, l, 0, e)))
            if even:
                to_mix = first_weights(m, out_slots, w_out)
                stages.append((f"proj{l}", lambda j=j: even_project(nc, s, m, a, j)))
                stages.append((f"gates{l}", lambda l=l: even_gates(nc, s, m, a, l)))
                stages.append((f"hgrn{l}", lambda j=j: hgrn(nc, s, m, a, out, j)))
                stages.append((f"post{l}", lambda j=j, e=to_mix: hgrn_norm(nc, s, m, a, j, e)))
            else:
                def to_mix(sp, w=w_out, slot=out_slots[0]):
                    m.early.load(sp, 0, slot, columns(w, 0))

                stages.append((f"proj{l}", lambda j=j: odd_project(nc, s, m, a, out, j)))
                stages.append((f"heads{l}", lambda j=j, l=l: odd_heads(nc, s, m, a, out, j, l)))
                stages.append((f"attention{l}", lambda j=j, e=to_mix: attention(nc, s, m, a, j, e)))
            stages.append((f"mix{l}", lambda l=l, w=w_out: out_project(nc, s, m, w, l)))
            to_peer = first_queries(s, m, a, l)
            stages.append((f"mod{l}1", lambda l=l, e=to_peer: modulate(nc, s, m, a, l, 1, e)))
            stages.append((f"peerq{l}", lambda l=l: peer_queries(nc, s, m, a, l)))
            stages.append((f"peer{l}", lambda l=l: peer(nc, s, m, a, l)))
        stages.append(("final", lambda: final_norm(nc, s, m, a, out)))
        for name, stage in stages:
            stage()
            if name == stop:
                dump(nc, s, m)
                return


ARENA = 30720


def setup(nc, s, m, a):
    with phase(nc, "landed const silu_ready raw_ready") as (block, S):
        raw = m.arena[:, 0:s.KD * 2].rearrange("p (k two) -> p k two", two=2)

        @block.sync
        def _(sp):
            sp.dma_start(m.x[:, 0, :], a.x_prompt[0]).then_inc(S.landed, 16)
            sp.dma_start(m.x[:, 1:s.T, :], a.x_sample[0].rearrange("(t p) d -> p t d", p=P)).then_inc(S.landed, 16)
            sp.wait_ge(S.landed, 32)

        @block.scalar
        def _(act):
            with nc.allow_non_contiguous_dma(reason="two short vectors"):
                act.dma_start(raw[:, :, 0], a.c_ctx.rearrange("(k p) -> p k", p=P)).then_inc(S.raw_ready, 16)
                act.dma_start(raw[:, :, 1], a.c[0].rearrange("(k p) -> p k", p=P)).then_inc(S.raw_ready, 16)
            act.wait_ge(S.raw_ready, 32)
            nc.scalar.activation(m.cT[:], raw, ACT.Silu).then_inc(S.silu_ready, 1)

        @block.gpsimd
        def _(pool):
            c = Chain(pool, S.const)
            c(pool.memset(m.eps[:], 1e-6))
            c(pool.memset(m.ones[:], 1.0))
            c(pool.memset(m.ident[:], 0.0))
            c(pool.affine_select(out=m.ident[:], in_=m.ident[:], compare_op=ALU.not_equal, fill=1.0, base=0,
                                 pattern=[[-1, P]], channel_multiplier=1))
            count = m.small[:, 0:16].bitcast(mybir.dt.int32)
            c(pool.iota(count, pattern=[[1, 16]], base=0, channel_multiplier=0))
            c(pool.tensor_copy(m.iota, count))
            c(pool.memset(m.pick[:], 0.0))
            c(pool.affine_select(out=m.pick[:], in_=m.pick[:], compare_op=ALU.not_equal, fill=1.0, base=0,
                                 pattern=[[-1, 2], [0, P]], channel_multiplier=1))


class ModRows:
    SLOTS = 5
    SEMS = f"rows_w_landed*{SLOTS} rows_bias_landed rows_full rows_fetched rows_biased "
    BANKS = 8

    def __init__(self, nc, s, m, a, l, half, S, weights, bias, raw, before=0):
        self.nc, self.s, self.m, self.S, self.half = nc, s, m, S, half
        self.w = a.w_mod[l].rearrange("(k p) (c n) -> p k c n", p=P, n=P)
        self.b = a.b_mod[l]
        self.ring, self.bias, self.raw = weights, bias, raw
        self.out = m.mod_rows[2 * l + half]
        self.K = s.KD // 2
        self.before = before
        self.chunks, self.groups = 2 * 3 * s.D // P, 3 * s.D // 512
        self.stores = m.stores
        m.stores += self.groups

    def load(self, sp):
        S, base = self.S, self.before * self.chunks
        c0 = self.half * 3 * self.s.D
        if self.before:
            sp.wait_ge(self.m.rows_stored, 16 * self.stores)
        sp.dma_start(self.bias, self.b[c0:c0 + 3 * self.s.D].partition_broadcast(2)).then_inc(S.rows_bias_landed, 16)
        for i in range(self.chunks):
            c, k0, slot = c0 // P + i // 2, i % 2 * self.K, (base + i) % self.SLOTS
            if base + i >= self.SLOTS:
                sp.wait_ge(S.rows_full, base + i - self.SLOTS + 1)
            sp.dma_start(self.ring[:, slot], self.w[:, k0:k0 + self.K, c]).then_inc(S.rows_w_landed[slot], 16)

    def multiply(self, pe):
        S, base = self.S, self.before * self.chunks
        for i in range(self.chunks):
            c, k0, g, slot = i // 2, i % 2 * self.K, i // 8, (base + i) % self.SLOTS
            pe.wait_ge(S.rows_w_landed[slot], 16 * ((base + i) // self.SLOTS + 1))
            at = self.before * self.groups + g
            if i % 8 == 0 and at >= self.BANKS:
                pe.wait_ge(S.rows_fetched, at - self.BANKS + 1)
            for k in range(self.K):
                mm = pe.matmul(self.m.ps[0:2, at % self.BANKS, c % 4 * P:(c % 4 + 1) * P], self.m.cT[:, k0 + k, :],
                               self.ring[:, slot, k, :], start=(k0 + k == 0), stop=(k0 + k == self.s.KD - 1))
            mm.then_inc(S.rows_full, 1)

    def fetch(self, act):
        S = self.S
        for g in range(self.groups):
            at = self.before * self.groups + g
            act.wait_ge(S.rows_full, self.before * self.chunks + 8 * (g + 1))
            if at >= 1:
                act.wait_ge(S.rows_biased, at)
            self.nc.scalar.activation(self.raw, self.m.ps[0:2, at % self.BANKS, :], ACT.Copy).then_inc(S.rows_fetched, 1)

    def finish(self, pool):
        S = self.S
        pool.wait_ge(S.rows_bias_landed, 16 * (self.before + 1))
        for g in range(self.groups):
            cols = slice(g * 512, (g + 1) * 512)
            pool.wait_ge(S.rows_fetched, self.before * self.groups + g + 1)
            pool.tensor_tensor(self.bias[:, cols], self.raw, self.bias[:, cols], ALU.add)\
                .then_inc(S.rows_biased, 1)
            pool.wait_ge(S.rows_biased, self.before * self.groups + g + 1)
            pool.dma_start(self.out[:, cols], self.bias[:, cols]).then_inc(self.m.rows_stored, 16)
        pool.wait_ge(self.m.rows_stored, 16 * (self.stores + self.groups))


def modulate(nc, s, m, a, l, half, early):
    D, KD, T = s.D, s.KD, s.T
    gain = m.arena[:, ARENA - D:ARENA]
    square = m.arena[:, ARENA - 2 * D:ARENA - D]
    sumsq, std, rstd = m.small[:, 0:T], m.small[:, 8:8 + T], m.small[:, 16:16 + T]
    gain_src = (a.norm1_g if half == 0 else a.norm2_g)[l]
    G = KD // 4
    with phase(nc, "rows_landed gain_landed gate_landed chain_a chain_v std_ready scaled h_ready hT_full "
                   "hT_used") as (block, S):
        @block.sync
        def _(sp):
            rows = m.mod_rows[2 * l + half]
            sp.dma_start(gain, gain_src.partition_broadcast(P)).then_inc(S.gain_landed, 16)
            for st in range(2):
                sp.dma_start(m.scale[:, st], rows[st, D:2 * D].partition_broadcast(P)).then_inc(S.rows_landed, 16)
            for st in range(2):
                sp.dma_start(m.shift[:, st], rows[st, 0:D].partition_broadcast(P)).then_inc(S.rows_landed, 16)
            for st in range(2):
                sp.dma_start(m.gate[:, st], rows[st, 2 * D:3 * D].partition_broadcast(P)).then_inc(S.gate_landed, 16)
            early(sp)
            sp.wait_ge(S.gate_landed, 32)

        @block.scalar
        def _(act):
            c = Chain(act, S.chain_a)
            for t in range(T):
                c(nc.scalar.activation(square, m.x[:, t, :], ACT.Square, accum_out=sumsq[:, t:t + 1]))
            nc.scalar.activation(std, sumsq, ACT.Sqrt, scale=1.0 / D, bias=m.eps[:]).then_inc(S.std_ready, 1)
            for i in range(T * G):
                t, g = divmod(i, G)
                act.wait_ge(S.hT_full, i + 1)
                nc.scalar.activation(m.hT[:, 4 * g:4 * g + 4, t * P:(t + 1) * P],
                                     m.ps[:, i % 8, :].rearrange("p (j n) -> p j n", j=4),
                                     ACT.Copy).then_inc(S.hT_used, 1)

        @block.tensor
        def _(pe):
            for i in range(T * G):
                t, g = divmod(i, G)
                pe.wait_ge(S.h_ready, t + 1)
                if i >= 8:
                    pe.wait_ge(S.hT_used, i - 7)
                for j in range(4):
                    k = 4 * g + j
                    mm = pe.transpose(m.ps[:, i % 8, j * P:(j + 1) * P], m.h[:, t, k * P:(k + 1) * P], m.ident[:])
                mm.then_inc(S.hT_full, 1)

        @block.vector
        def _(dve):
            c = Chain(dve, S.chain_v)
            dve.wait_ge(S.rows_landed, 64)
            dve.wait_ge(S.gain_landed, 16)
            for st in range(2):
                dve.scalar_tensor_tensor(m.scale[:, st], m.scale[:, st], 1.0, gain, ALU.add, ALU.mult)\
                    .then_inc(S.scaled, 1)
            dve.wait_ge(S.scaled, 2)
            dve.wait_ge(S.std_ready, 1)
            c(dve.reciprocal(rstd, std))
            for t in range(T):
                st = min(t, 1)
                c(dve.scalar_tensor_tensor(m.h[:, t, :], m.x[:, t, :], rstd[:, t:t + 1], m.scale[:, st, :],
                                           ALU.mult, ALU.mult))
                dve.tensor_tensor(m.h[:, t, :], m.h[:, t, :], m.shift[:, st, :], ALU.add).then_inc(S.h_ready, 1)


def modulation(nc, s, m, a, l, half, early):
    D, KD, T = s.D, s.KD, s.T
    NCH = 3 * D // 512
    per_row = D // 512
    ring = m.arena[:, 0:2 * KD * 512].rearrange("p (b k n) -> p b k n", b=2, k=KD)
    at = 2 * KD * 512
    bias = m.arena[0:2, at:at + 3 * D]
    rows = m.arena[0:2, at + 3 * D:at + 6 * D]
    gain = m.arena[:, at + 6 * D:at + 7 * D]
    square = m.hT[:].rearrange("p k n -> p (k n)")[:, 0:D]
    sumsq = m.small[:, 0:T]
    std = m.small[:, 8:8 + T]
    rstd = m.small[:, 16:16 + T]
    gain_src = (a.norm1_g if half == 0 else a.norm2_g)[l]
    dest = [m.shift, m.scale, m.gate]
    with phase(nc, "w_landed*2 bias_landed gain_landed rows_full row_ready wide_full wide_used chain_a chain_v "
                   "std_ready h_ready hT_full hT_used") as (block, S):
        @block.sync
        def _(sp):
            c0 = half * 3 * D
            for n in range(NCH):
                if n >= 2:
                    sp.wait_ge(S.rows_full, n - 1)
                src = a.w_mod[l][:, c0 + n * 512:c0 + (n + 1) * 512].rearrange("(k p) n -> p k n", p=P)
                sp.dma_start(ring[:, n % 2], src).then_inc(S.w_landed[n % 2], 16)
                if n == 0:
                    sp.dma_start(bias, a.b_mod[l][c0:c0 + 3 * D].partition_broadcast(2)).then_inc(S.bias_landed, 16)
                    sp.dma_start(gain, gain_src.partition_broadcast(P)).then_inc(S.gain_landed, 16)
            early(sp)

        @block.tensor
        def _(pe):
            def wide(n):
                pe.wait_ge(S.row_ready, n + 1)
                for st in range(2):
                    i = 2 * n + st
                    if i >= 4:
                        pe.wait_ge(S.wide_used, i - 3)
                    pe.matmul(m.ps[:, 2 + i % 4, :], m.pick[:, st, :], rows[:, n * 512:(n + 1) * 512],
                              start=True, stop=True).then_inc(S.wide_full, 1)

            for n in range(NCH):
                pe.wait_ge(S.w_landed[n % 2], 16 * (n // 2 + 1))
                if n >= 2:
                    pe.wait_ge(S.row_ready, n - 1)
                for k in range(KD):
                    mm = pe.matmul(m.ps[0:2, n % 2, :], m.cT[:, k, :], ring[:, n % 2, k, :],
                                   start=(k == 0), stop=(k == KD - 1))
                mm.then_inc(S.rows_full, 1)
                if n >= 1:
                    wide(n - 1)
            wide(NCH - 1)
            for t in range(T):
                pe.wait_ge(S.h_ready, t + 1)
                for g in range(KD // 4):
                    i = t * (KD // 4) + g
                    if i >= 2:
                        pe.wait_ge(S.hT_used, i - 1)
                    for j in range(4):
                        k = 4 * g + j
                        mm = pe.transpose(m.ps[:, 6 + i % 2, j * P:(j + 1) * P], m.h[:, t, k * P:(k + 1) * P],
                                          m.ident[:])
                    mm.then_inc(S.hT_full, 1)

        @block.scalar
        def _(act):
            c = Chain(act, S.chain_a)
            for t in range(T):
                c(nc.scalar.activation(square, m.x[:, t, :], ACT.Square, accum_out=sumsq[:, t:t + 1]))
            nc.scalar.activation(std, sumsq, ACT.Sqrt, scale=1.0 / D, bias=m.eps[:]).then_inc(S.std_ready, 1)
            for i in range(T * (KD // 4)):
                t, g = divmod(i, KD // 4)
                act.wait_ge(S.hT_full, i + 1)
                nc.scalar.activation(m.hT[:, 4 * g:4 * g + 4, t * P:(t + 1) * P],
                                     m.ps[:, 6 + i % 2, :].rearrange("p (j n) -> p j n", j=4),
                                     ACT.Copy).then_inc(S.hT_used, 1)

        @block.vector
        def _(dve):
            c = Chain(dve, S.chain_v)

            def widened(n):
                row, col = divmod(n, per_row)
                for st in range(2):
                    i = 2 * n + st
                    dve.wait_ge(S.wide_full, i + 1)
                    d = dest[row][:, st, col * 512:(col + 1) * 512]
                    p = m.ps[:, 2 + i % 4, :]
                    if row == 1:
                        dve.scalar_tensor_tensor(d, p, 1.0, gain[:, col * 512:(col + 1) * 512], ALU.add,
                                                 ALU.mult).then_inc(S.wide_used, 1)
                    else:
                        dve.tensor_copy(d, p).then_inc(S.wide_used, 1)

            dve.wait_ge(S.bias_landed, 16)
            dve.wait_ge(S.gain_landed, 16)
            for n in range(NCH):
                dve.wait_ge(S.rows_full, n + 1)
                dve.tensor_tensor(rows[:, n * 512:(n + 1) * 512], m.ps[0:2, n % 2, :],
                                  bias[:, n * 512:(n + 1) * 512], ALU.add).then_inc(S.row_ready, 1)
                if n >= 1:
                    widened(n - 1)
            widened(NCH - 1)
            dve.wait_ge(S.wide_used, 2 * NCH)
            dve.wait_ge(S.std_ready, 1)
            c(dve.reciprocal(rstd, std))
            for t in range(T):
                st = min(t, 1)
                c(dve.scalar_tensor_tensor(m.h[:, t, :], m.x[:, t, :], rstd[:, t:t + 1], m.scale[:, st, :],
                                           ALU.mult, ALU.mult))
                dve.tensor_tensor(m.h[:, t, :], m.h[:, t, :], m.shift[:, st, :], ALU.add).then_inc(S.h_ready, 1)


def evacuate_alternately(engine_name, i):
    return (i % 2 == 0) == (engine_name == "scalar")


def weights_there(pe, m, S, n):
    if n < 2:
        m.early.wait(pe, n)
    else:
        pe.wait_ge(S.w_landed[n % 2], 16 * (n // 2))


def even_slots(s, m):
    return two_slots(m, s, (PJ_WORDS, PJ_WORDS + s.KD * 512))


def first_weights(m, slots, w):
    def early(sp):
        for i in range(2):
            m.early.load(sp, i, slots[i], columns(w, i))
    return early


def even_project(nc, s, m, a, j):
    KD, T, N = s.KD, s.T, s.N
    w = a.even_w_in[j]
    LF = 3 + 3
    LOADS = w.shape[1] // 512
    ring = even_slots(s, m)
    PJ = m.arena[:, 0:PJ_WORDS].rearrange("p (c n) -> p c n", n=N)
    with phase(nc, "w_landed*2 full used_scalar used_vector") as (block, S):
        def fills():
            i = 0
            for n in range(LF):
                for c in range(4):
                    yield i, (n, c)
                    i += 1
            for n in range(LF, LOADS):
                for t in range(T):
                    yield i, (n, t)
                    i += 1

        def place(i, n, c):
            if n < LF:
                b = 2 * (i % 4)
                src = m.ps[:, b:b + 2, :].rearrange("p b n -> p (b n)")[:, 0:N]
                return b, src, PJ[:, 4 * n + c, :]
            b = 2 * (i % 4)
            return b, m.ps[:, b, :], VO(m, s)[:, c, (n - LF) * 512:(n - LF + 1) * 512]

        @block.sync
        def _(sp):
            for n in range(2, LOADS):
                sp.wait_ge(S.full, max(i for i, (load, _) in fills() if load == n - 2) + 1)
                sp.dma_start(ring[n % 2], columns(w, n)).then_inc(S.w_landed[n % 2], 16)

        @block.tensor
        def _(pe):
            last = -1
            for i, (n, c) in fills():
                if n != last:
                    weights_there(pe, m, S, n)
                    last = n
                if i >= 4:
                    pe.wait_ge(S.used_scalar if i % 2 == 0 else S.used_vector, (i - 4) // 2 + 1)
                b, _, _ = place(i, n, c)
                for k in range(KD):
                    first, end = k == 0, k == KD - 1
                    if n < LF:
                        lhsT = ring[n % 2][:, k, c * P:(c + 1) * P]
                        pe.matmul(m.ps[:, b, :], lhsT, m.hT[:, k, 0:512], start=first, stop=end)
                        mm = pe.matmul(m.ps[:, b + 1, 0:N - 512], lhsT, m.hT[:, k, 512:N], start=first, stop=end)
                    else:
                        mm = pe.matmul(m.ps[:, b, :], m.hT[:, k, c * P:(c + 1) * P], ring[n % 2][:, k, :],
                                       start=first, stop=end)
                mm.then_inc(S.full, 1)

        @block.scalar
        def _(act):
            for i, (n, c) in fills():
                if i % 2 == 0:
                    act.wait_ge(S.full, i + 1)
                    _, src, dst = place(i, n, c)
                    nc.scalar.activation(dst, src, ACT.Copy).then_inc(S.used_scalar, 1)

        @block.vector
        def _(dve):
            for i, (n, c) in fills():
                if i % 2 == 1:
                    dve.wait_ge(S.full, i + 1)
                    _, src, dst = place(i, n, c)
                    dve.tensor_copy(dst, src).then_inc(S.used_vector, 1)


PJ_WORDS = 24 * 640


def VO(m, s):
    return m.h[:]


XE_AT = PJ_WORDS
XE_WORDS = 8 * 5 * (P + 1)
GA_AT = XE_AT + XE_WORDS
LEVELS = 7
GA_WORDS = LEVELS * 640
S0_AT = GA_AT + 2 * GA_WORDS


def even_views(s, m):
    v = Memory()
    PJ = m.arena[:, 0:PJ_WORDS].rearrange("p (c n) -> p c n", n=s.N)
    v.gb, v.gated_by, v.u, v.q, v.z = PJ[:, 0:4], PJ[:, 4:8], PJ[:, 8:12], PJ[:, 12:16], PJ[:, 16:24]
    v.kk = PJ[:, 0:8]
    v.o = m.arena[:, 8 * s.N:12 * s.N].rearrange("p (t h v) -> p t h v", t=s.T, h=s.H)
    v.XE = m.arena[:, XE_AT:XE_AT + XE_WORDS].rearrange("p (c t n) -> p c t n", c=8, t=s.T)
    v.GA = m.arena[:, GA_AT:GA_AT + 2 * GA_WORDS].rearrange("p (b l n) -> p b l n", b=2, l=LEVELS)
    z0 = 16 * s.N
    v.GB = m.arena[:, z0:z0 + 4 * s.N].rearrange("p (b e n) -> p b e n", b=2, e=2)
    z0 += 4 * s.N
    v.S = m.arena[:, z0:z0 + 2 * s.T * P].rearrange("p (d t v) -> p d t v", d=2, t=s.T)
    z0 += 2 * s.T * P
    v.kdT = m.arena[:, z0:z0 + 4 * P].rearrange("p (j k) -> p j k", j=4)
    v.s0 = m.arena[:, S0_AT:S0_AT + 8 * P].rearrange("p (c v) -> p c v", c=8)
    v.masks = m.shift[:].rearrange("p s (e t) -> p s e t", t=P)
    v.masked = m.scale[:].rearrange("p s (e t) -> p s e t", t=P)
    v.conv_w = m.small[:, 32:44].rearrange("p (j c) -> p j c", j=3)
    v.lb_raw = m.small[:, 48:72].rearrange("p (k c) -> p k c", k=3)
    v.lb, v.oml, v.lb_max = m.small[:, 72:80], m.small[:, 80:88], m.small[:, 88:96]
    v.decay = m.small[:, 96:136].rearrange("p (c t) -> p c t", c=8)
    return v


def even_gates(nc, s, m, a, l):
    v = even_views(s, m)
    j, T, N = l // 2, s.T, s.N
    SEG = N + 4
    pad = m.arena[:, XE_AT:XE_AT + 4 * SEG].rearrange("p (c n) -> p c n", c=4)
    acc = m.arena[:, GA_AT:GA_AT + 4 * (SEG - 2)].rearrange("p (c n) -> p c n", c=4)
    spans = [(0, 0, P), (P, P + 2, N - P)]
    sgn = m.arena[:, GA_AT:GA_AT + 8 * N].rearrange("p (c n) -> p c n", c=8)
    with phase(nc, ModRows.SEMS + "small_landed masks_landed chain_v chain_a shifted exp_ready sig_ready conv_done "
                                  "forget_ready log_ready") as (block, S):
        weights = m.hT[:, 4:8, :].rearrange("p k n -> p (k n)")\
            .rearrange("p (b k n) -> p b k n", b=ModRows.SLOTS, n=P)
        at = GA_AT + 8 * N
        bias, raw = m.arena[0:2, at:at + 3 * s.D], m.arena[0:2, at + 3 * s.D:at + 3 * s.D + 512]
        made = [ModRows(nc, s, m, a, l + (i + 1) // 2, (i + 1) % 2, S, weights, bias, raw, i)
                for i in range(2) if l + (i + 1) // 2 < s.DEPTH]

        @block.tensor
        def _(pe):
            for rows in made:
                rows.multiply(pe)

        @block.gpsimd
        def _(pool):
            for rows in made:
                rows.finish(pool)

        @block.sync
        def _(sp):
            sp.dma_start(v.masks, a.hgrn_masks).then_inc(S.masks_landed, 16)
            with nc.allow_non_contiguous_dma(reason="per-channel weights, short"):
                for i in range(3):
                    sp.dma_start(v.conv_w[:, i], a.even_conv_w[j, i].rearrange("(c p) -> p c", p=P))\
                        .then_inc(S.small_landed, 16)
                    for d in range(2):
                        sp.dma_start(v.lb_raw[:, i, 4 * d:4 * d + 4],
                                     a.lb_logits[i, d].rearrange("(c p) -> p c", p=P)).then_inc(S.small_landed, 16)
            sp.dma_start(v.s0, a.state_hgrn[0, j].rearrange("d h k v -> k (d h) v")).then_inc(S.masks_landed, 16)
            for rows in made:
                rows.load(sp)
            sp.wait_ge(S.masks_landed, 32)

        @block.vector
        def _(dve):
            c = Chain(dve, S.chain_v)
            dve.wait_ge(S.small_landed, 9 * 16)
            c(dve.tensor_tensor(v.lb_max, v.lb_raw[:, 0], v.lb_raw[:, 1], ALU.max))
            c(dve.tensor_tensor(v.lb_max, v.lb_max, v.lb_raw[:, 2], ALU.max))
            dve.tensor_tensor(v.lb_raw, v.lb_raw, v.lb_max.unsqueeze(1).to_broadcast([P, 3, 8]), ALU.subtract)\
                .then_inc(S.shifted, 1)
            for at in (0, P + 1, P + 2, SEG - 1):
                c(dve.memset(pad[:, :, at:at + 1], 0.0))
            for t0, at, n in spans:
                c(dve.tensor_tensor(pad[:, :, at + 1:at + 1 + n], v.gated_by[:, :, t0:t0 + n], v.u[:, :, t0:t0 + n],
                                    ALU.mult))
            for ch in range(4):
                c(dve.tensor_scalar(acc[:, ch], pad[:, ch, 0:SEG - 2], v.conv_w[:, 0, ch:ch + 1], None, ALU.mult))
                for i in (1, 2):
                    c(dve.scalar_tensor_tensor(acc[:, ch], pad[:, ch, i:i + SEG - 2], v.conv_w[:, i, ch:ch + 1],
                                               acc[:, ch], ALU.mult, ALU.add))
            for t0, at, n in spans:
                c(dve.tensor_tensor(m.hT[:, 0:4, t0:t0 + n], acc[:, :, at:at + n], v.gb[:, :, t0:t0 + n], ALU.mult))
            dve.sem_inc(S.conv_done, 1)
            dve.wait_ge(S.exp_ready, 1)
            c(dve.tensor_tensor(v.oml, v.lb_raw[:, 0], v.lb_raw[:, 1], ALU.add))
            c(dve.tensor_tensor(v.oml, v.oml, v.lb_raw[:, 2], ALU.add))
            c(dve.reciprocal(v.oml, v.oml))
            c(dve.tensor_copy(v.lb, v.lb_raw[:, 0]))
            for i in range(1, l + 1):
                c(dve.tensor_tensor(v.lb, v.lb, v.lb_raw[:, i], ALU.add))
            c(dve.tensor_tensor(v.lb, v.lb, v.oml, ALU.mult))
            c(dve.tensor_scalar(v.oml, v.lb, -1.0, 1.0, ALU.mult, ALU.add))
            dve.wait_ge(S.sig_ready, 2)
            for ch in range(8):
                c(dve.tensor_scalar(v.z[:, ch], v.z[:, ch], v.oml[:, ch:ch + 1], v.lb[:, ch:ch + 1], ALU.mult,
                                    ALU.add))
            dve.sem_inc(S.forget_ready, 1)
            for ch in range(8):
                c(dve.tensor_scalar(v.kk[:, ch], sgn[:, ch], v.oml[:, ch:ch + 1], None, ALU.mult))
            c(dve.memset(v.XE[:, :, :, 0:1], 0.0))
            dve.wait_ge(S.log_ready, 1)
            for ch in range(8):
                for t in range(T):
                    c(dve.tensor_tensor_scan(v.XE[:, ch, t, 1:P + 1], m.ones[:], v.z[:, ch, t * P:(t + 1) * P], 0.0,
                                             ALU.mult, ALU.add))

        @block.scalar
        def _(act):
            c = Chain(act, S.chain_a)
            c(nc.scalar.activation(v.q, v.q, ACT.Silu))
            act.wait_ge(S.shifted, 1)
            nc.scalar.activation(v.lb_raw, v.lb_raw, ACT.Exp).then_inc(S.exp_ready, 1)
            act.wait_ge(S.conv_done, 1)
            nc.scalar.activation(sgn, v.z, ACT.Sigmoid, scale=-1.0).then_inc(S.sig_ready, 1)
            act.wait_ge(S.sig_ready, 1)
            nc.scalar.activation(v.z, v.z, ACT.Sigmoid).then_inc(S.sig_ready, 1)
            act.wait_ge(S.forget_ready, 1)
            nc.scalar.activation(v.z, v.z, ACT.Ln).then_inc(S.log_ready, 1)
            for rows in made:
                rows.fetch(act)


def hgrn(nc, s, m, a, out, j):
    v = even_views(s, m)
    T, N, H = s.T, s.N, s.H
    UNITS = 2 * H
    PARTS = [(0, 3), (3, 5), (5, LEVELS)]
    EXPS = len(PARTS) + 2
    FOLD = (LEVELS + 1) // 2
    values = VO(m, s)
    order = [[1, 2, 3, 0], [4, 3, 2, 0]]
    assert s.TS == 4
    first = [1, 4]

    def of(u):
        return u // 2, u % 2

    def where(u, piece):
        return (0 if piece == "q" else 1) if of(u)[1] == 0 else (1 if piece == "q" else 0)

    with phase(nc, "chain_v diffs_ready exp_ready decay_ready edges_ready levels_ready kT_full kT_used pair_full "
                   "masked delta_full state_ready state_out*2 o_full o_added o_copied") as (block, S):
        def X(u):
            h, d = of(u)
            return v.XE[:, 4 * d + h]

        def halves(ap, w):
            r = ap.rearrange("p t (g w) -> p t g w", w=2 * w)
            return r[:, :, :, 0:w], r[:, :, :, w:2 * w]

        def tiled(ap):
            return ap.rearrange("p (t n) -> p t n", n=P)

        @block.gpsimd
        def _(pool):
            def differences(u):
                h, d = of(u)
                off, b = 1 - d, u % 2
                if u >= 2:
                    pool.wait_ge(S.pair_full, T * (u - 1))
                x = X(u)
                for lv in range(LEVELS):
                    w = P >> (lv + 1)
                    g = P // (2 * w)
                    left, right = halves(x[:, :, off:off + P], w)
                    gl, gr = halves(tiled(v.GA[:, b, lv]), w)
                    R = x[:, :, w:w + (g - 1) * 2 * w + 1:2 * w].unsqueeze(3).to_broadcast([P, T, g, w])
                    pool.tensor_tensor(gl, R, left, ALU.subtract).then_inc(S.diffs_ready, 1)
                    pool.tensor_tensor(gr, right, R, ALU.subtract).then_inc(S.diffs_ready, 1)
                if u >= 2:
                    pool.wait_ge(S.o_full, T * (u - 1))
                last = x[:, :, P:P + 1].to_broadcast([P, T, P])
                pool.tensor_tensor(tiled(v.GB[:, b, 1]), last, x[:, :, off:off + P], ALU.subtract)\
                    .then_inc(S.diffs_ready, 1)

            for u in range(UNITS):
                differences(u)

        @block.vector
        def _(dve):
            c = Chain(dve, S.chain_v)

            def products(u):
                h, d = of(u)
                b = u % 2
                q, k = v.q[:, h], v.kk[:, 4 * d + h]
                early, late = (k, q) if d == 0 else (q, k)
                for lv in range(LEVELS):
                    part = [l0 for l0, _ in PARTS]
                    if lv in part:
                        dve.wait_ge(S.exp_ready, EXPS * u + part.index(lv) + 1)
                    w = P >> (lv + 1)
                    gl, gr = halves(tiled(v.GA[:, b, lv]), w)
                    dve.tensor_tensor(gl, gl, halves(tiled(early), w)[0], ALU.mult).then_inc(S.levels_ready, 1)
                    dve.tensor_tensor(gr, gr, halves(tiled(late), w)[1], ALU.mult).then_inc(S.levels_ready, 1)
                dve.wait_ge(S.exp_ready, EXPS * (u + 1))
                for piece, src in (("q", q), ("k", k)):
                    g = v.GB[:, b, where(u, piece)]
                    dve.tensor_tensor(g, g, src, ALU.mult).then_inc(S.edges_ready, 1)

            def states(u):
                h, d = of(u)
                if u >= 2:
                    dve.wait_ge(S.o_full, T * (u - 1))
                    dve.wait_ge(S.state_out[d], 16 * (u // 2))
                dve.wait_ge(S.delta_full, u + 1)
                dve.wait_ge(S.decay_ready, 1)
                prev = v.s0[:, 4 * d + h]
                for i, t in enumerate(order[d][:3]):
                    nxt = order[d][i + 1] if i < 2 else (4 if d == 0 else 1)
                    dve.scalar_tensor_tensor(v.S[:, d, nxt], prev, v.decay[:, 4 * d + h, t:t + 1],
                                             m.ps[:, 5, i * P:(i + 1) * P], ALU.mult, ALU.add)\
                        .then_inc(S.state_ready, 1)
                    dve.wait_ge(S.state_ready, 4 * u + i + 1)
                    prev = v.S[:, d, nxt]
                dve.tensor_copy(v.S[:, d, 0], m.ps[:, 5, 3 * P:4 * P]).then_inc(S.state_ready, 1)

            def mask(u, t):
                i = T * u + t
                dve.wait_ge(S.pair_full, i + 1)
                if i >= 2:
                    dve.wait_ge(S.o_full, i - 1)
                pairs = m.ps[:, 2 * (i % 2):2 * (i % 2) + 2, :].rearrange("p b (e t) -> p (b e) t", t=P)
                c(dve.tensor_tensor(v.masked[:, i % 2], pairs, v.masks[:, of(u)[1]], ALU.mult))
                lower, upper = v.masked[:, i % 2, 0:FOLD], v.masked[:, i % 2, FOLD:2 * FOLD]
                dve.tensor_tensor(lower, lower, upper, ALU.add).then_inc(S.masked, 1)

            products(0)
            for u in range(UNITS):
                h, d = of(u)
                mask(u, 0)
                states(u)
                mask(u, 1)
                mask(u, 2)
                if u + 1 < UNITS:
                    products(u + 1)
                mask(u, 3)
                mask(u, 4)
                if d == 1:
                    dve.wait_ge(S.o_full, T * (u + 1))
                    dve.wait_ge(S.o_copied, h + 1)
                    dve.tensor_tensor(v.o[:, 1:T, h], v.o[:, 1:T, h],
                                      m.ps[:, 6, :].rearrange("p (t n) -> p t n", n=P), ALU.add)\
                        .then_inc(S.o_added, 1)
                    dve.tensor_tensor(v.o[:, 0, h], v.o[:, 0, h], m.ps[:, 7, 0:P], ALU.add).then_inc(S.o_added, 1)

        @block.scalar
        def _(act):
            def exps(u):
                b, (h, d) = u % 2, of(u)
                n = (2 * LEVELS + 1) * u
                off = 1 - d
                for l0, l1 in PARTS:
                    act.wait_ge(S.diffs_ready, n + 2 * l1)
                    nc.scalar.activation(v.GA[:, b, l0:l1], v.GA[:, b, l0:l1], ACT.Exp).then_inc(S.exp_ready, 1)
                if u >= 2:
                    act.wait_ge(S.o_full, T * (u - 1))
                nc.scalar.activation(tiled(v.GB[:, b, 0]), X(u)[:, :, off:off + P], ACT.Exp).then_inc(S.exp_ready, 1)
                act.wait_ge(S.diffs_ready, n + 1 + 2 * LEVELS)
                nc.scalar.activation(v.GB[:, b, 1], v.GB[:, b, 1], ACT.Exp).then_inc(S.exp_ready, 1)

            nc.scalar.activation(v.decay, v.XE[:, :, :, P], ACT.Exp).then_inc(S.decay_ready, 1)
            exps(0)
            for u in range(UNITS):
                h, d = of(u)
                act.wait_ge(S.kT_full, u + 1)
                if u >= 1:
                    act.wait_ge(S.delta_full, u)
                nc.scalar.activation(v.kdT, m.ps[:, 4, :].rearrange("p (j k) -> p j k", j=4), ACT.Copy)\
                    .then_inc(S.kT_used, 1)
                if u + 1 < UNITS:
                    exps(u + 1)
                if d == 0:
                    act.wait_ge(S.o_full, T * (u + 1))
                    nc.scalar.activation(v.o[:, 1:T, h], m.ps[:, 6, :].rearrange("p (t n) -> p t n", n=P), ACT.Copy)
                    nc.scalar.activation(v.o[:, 0, h], m.ps[:, 7, 0:P], ACT.Copy).then_inc(S.o_copied, 1)

        @block.sync
        def _(sp):
            for u in range(UNITS):
                h, d = of(u)
                sp.wait_ge(S.state_ready, 4 * (u + 1))
                sp.dma_start(out.state[j, d, h], v.S[:, d, 0]).then_inc(S.state_out[d], 16)
            for d in range(2):
                sp.wait_ge(S.state_out[d], 16 * H)

        @block.tensor
        def _(pe):
            for u in range(UNITS):
                (h, d), b = of(u), u % 2
                tile = lambda ap, t: ap[:, t * P:(t + 1) * P]
                kd, qd = v.GB[:, b, where(u, "k")], v.GB[:, b, where(u, "q")]

                def pairs(t):
                    i = T * u + t
                    if i >= 2:
                        pe.wait_ge(S.masked, i - 1)
                    for e in range(LEVELS + 1):
                        dst = m.ps[:, 2 * (i % 2) + e // 4, (e % 4) * P:(e % 4 + 1) * P]
                        if e < LEVELS:
                            g = tile(v.GA[:, b, e], t)
                            mm = pe.matmul(dst, g, g, start=True, stop=True)
                        else:
                            mm = pe.matmul(dst, tile(v.kk[:, 4 * d + h], t), tile(v.q[:, h], t), start=True,
                                           stop=True)
                    mm.then_inc(S.pair_full, 1)

                pe.wait_ge(S.levels_ready, 2 * LEVELS * (u + 1))
                pairs(0)
                pe.wait_ge(S.edges_ready, 2 * (u + 1))
                if u >= 1:
                    pe.wait_ge(S.kT_used, u)
                for i, t in enumerate(order[d]):
                    mm = pe.transpose(m.ps[:, 4, i * P:(i + 1) * P], tile(kd, t), m.ident[:])
                mm.then_inc(S.kT_full, 1)
                pairs(1)
                pe.wait_ge(S.kT_used, u + 1)
                if u >= 1:
                    pe.wait_ge(S.state_ready, 4 * u)
                for i, t in enumerate(order[d]):
                    mm = pe.matmul(m.ps[:, 5, i * P:(i + 1) * P], v.kdT[:, i], values[:, t, h * P:(h + 1) * P],
                                   start=True, stop=True)
                mm.then_inc(S.delta_full, 1)
                for t in range(T):
                    i = T * u + t
                    if 1 <= t and t + 1 < T:
                        pairs(t + 1)
                    pe.wait_ge(S.masked, i + 1)
                    if t == 0 and u >= 1:
                        if d == 1:
                            pe.wait_ge(S.o_copied, h + 1)
                        else:
                            pe.wait_ge(S.o_added, 2 * h)
                    if t == 1:
                        pe.wait_ge(S.state_ready, 4 * (u + 1))
                    dst = m.ps[:, 7, 0:P] if t == 0 else m.ps[:, 6, (t - 1) * P:t * P]
                    for e in range(FOLD):
                        mm = pe.matmul(dst, v.masked[:, i % 2, e], values[:, t, h * P:(h + 1) * P],
                                       start=(e == 0), stop=(e == FOLD - 1 and t == 0))
                    if t > 0:
                        state = v.s0[:, 4 * d + h] if t == first[d] else v.S[:, d, t]
                        mm = pe.matmul(dst, tile(qd, t), state, start=False, stop=True)
                    mm.then_inc(S.o_full, 1)


def hgrn_norm(nc, s, m, a, j, early):
    v = even_views(s, m)
    T, H = s.T, s.H
    o = v.o.rearrange("p t h v -> p (t h) v")
    gain = m.arena[:, GA_AT:GA_AT + H * P]
    squares = m.arena[:, GA_AT + 1024:GA_AT + 1024 + T * H * P].rearrange("p (c v) -> p c v", v=P)
    og = VO(m, s)[:, :, s.W2:2 * s.W2]
    sumsq, rstd = m.small[:, 0:T * H], m.small[:, T * H:2 * T * H]
    with phase(nc, "gain_landed chain_v sum_ready std_ready silu_ready o_ready full used") as (block, S):
        @block.sync
        def _(sp):
            sp.dma_start(gain, a.hgrn_onorm_g[j].partition_broadcast(P)).then_inc(S.gain_landed, 16)
            early(sp)

        @block.scalar
        def _(act):
            nc.scalar.activation(og, og, ACT.Silu).then_inc(S.silu_ready, 1)
            act.wait_ge(S.sum_ready, 1)
            nc.scalar.activation(rstd, sumsq, ACT.Sqrt, scale=1.0 / P, bias=m.eps[:]).then_inc(S.std_ready, 1)
            for t in range(T):
                act.wait_ge(S.full, t + 1)
                nc.scalar.activation(m.hT[:, 4:8, t * P:(t + 1) * P],
                                     m.ps[:, t % 2, :].rearrange("p (j n) -> p j n", j=4), ACT.Copy)\
                    .then_inc(S.used, 1)

        @block.vector
        def _(dve):
            c = Chain(dve, S.chain_v)
            c(dve.tensor_tensor(squares, o, o, ALU.mult))
            dve.tensor_reduce(sumsq, squares, AX.X, ALU.add).then_inc(S.sum_ready, 1)
            dve.wait_ge(S.std_ready, 1)
            c(dve.reciprocal(rstd, rstd))
            c(dve.tensor_tensor(o, o, rstd.unsqueeze(2).to_broadcast([P, T * H, P]), ALU.mult))
            dve.wait_ge(S.gain_landed, 16)
            dve.wait_ge(S.silu_ready, 1)
            for t in range(T):
                ot = v.o[:, t].rearrange("p h v -> p (h v)")
                c(dve.tensor_tensor(ot, ot, gain, ALU.mult))
                dve.tensor_tensor(ot, ot, og[:, t], ALU.mult).then_inc(S.o_ready, 1)

        @block.tensor
        def _(pe):
            for t in range(T):
                pe.wait_ge(S.o_ready, t + 1)
                if t >= 2:
                    pe.wait_ge(S.used, t - 1)
                for h in range(H):
                    mm = pe.transpose(m.ps[:, t % 2, h * P:(h + 1) * P], v.o[:, t, h], m.ident[:])
                mm.then_inc(S.full, 1)


def mix_slots(s, m, even):
    at = (8192, 8192 + s.KD * 512) if even else (ARENA - s.KD * 512, 0)
    return two_slots(m, s, at), m.arena[:, 17408:18432].rearrange("p (b n) -> p b n", b=2)


def out_project(nc, s, m, w, l):
    KD, T, D = s.KD, s.T, s.D
    LOADS = D // 512
    assert LOADS == 2
    slots, gated = mix_slots(s, m, l % 2 == 0)
    with phase(nc, "w_landed full gated added") as (block, S):
        if l % 2 == 1:
            @block.sync
            def _(sp):
                sp.dma_start(slots[1], columns(w, 1)).then_inc(S.w_landed, 16)

        @block.tensor
        def _(pe):
            for n in range(LOADS):
                if n == 1 and l % 2 == 1:
                    pe.wait_ge(S.w_landed, 16)
                else:
                    m.early.wait(pe, n)
                for t in range(T):
                    i = n * T + t
                    if i >= 8:
                        pe.wait_ge(S.gated, i - 7)
                    for k in range(KD):
                        mm = pe.matmul(m.ps[:, i % 8, :], m.hT[:, k, t * P:(t + 1) * P], slots[n][:, k, :],
                                       start=(k == 0), stop=(k == KD - 1))
                    mm.then_inc(S.full, 1)

        @block.vector
        def _(dve):
            for n in range(LOADS):
                for t in range(T):
                    i = n * T + t
                    cols = slice(n * 512, (n + 1) * 512)
                    dve.wait_ge(S.full, i + 1)
                    if i >= 2:
                        dve.wait_ge(S.added, i - 1)
                    dve.tensor_tensor(gated[:, i % 2], m.ps[:, i % 8, :], m.gate[:, min(t, 1), cols], ALU.mult)\
                        .then_inc(S.gated, 1)
                    dve.wait_ge(S.gated, i + 1)
                    dve.tensor_tensor(m.x[:, t, cols], m.x[:, t, cols], gated[:, i % 2], ALU.add)\
                        .then_inc(S.added, 1)


def wait(engine, sem, value):
    if isinstance(value, int) and value <= 0:
        return
    engine.wait_ge(sem, value)


def hold(engine, sem, value, step):
    wait(engine, sem, value)
    if not isinstance(value, int):
        engine.sem_inc(step, 1)


Q_WORDS = 16 * 640
U_AT = Q_WORDS
SLOTS = 8
V_AT = U_AT + SLOTS * 1024
HCUR_AT = V_AT + SLOTS * 1024
SEL_AT = HCUR_AT + 2 * 1024
TOPK = 16


def query_slots(s, m):
    at = U_AT + 2 * s.KD * 512
    return two_slots(m, s, (U_AT, U_AT + s.KD * 512)), \
        m.arena[:, at:at + 2 * s.HEADS * P].rearrange("p (c k) -> p c k", k=P)


def first_queries(s, m, a, l):
    slots, keys = query_slots(s, m)

    def early(sp):
        m.early.load(sp, 2, keys, a.peer_subkeys[l].rearrange("h s n k -> n (h s) k"))
        for i in range(2):
            m.early.load(sp, i, slots[i], columns(a.peer_w_q[l], i))
    return early


def peer_queries(nc, s, m, a, l):
    KD, N = s.KD, s.N
    w = a.peer_w_q[l]
    LOADS, SUB = w.shape[1] // 512, 2 * s.HEADS
    ring, keys = query_slots(s, m)
    queries = m.arena[:, 0:Q_WORDS].rearrange("p (c n) -> p c n", n=N)
    keysT = m.shift[:].rearrange("p s (c n) -> p (s c) n", n=P)
    with phase(nc, "w_landed*2 keysT_full keysT_used full used") as (block, S):
        @block.sync
        def _(sp):
            for n in range(2, LOADS):
                sp.wait_ge(S.full, n - 1)
                sp.dma_start(ring[n % 2], columns(w, n)).then_inc(S.w_landed[n % 2], 16)

        @block.tensor
        def _(pe):
            m.early.wait(pe, 2)
            for g in range(SUB // 4):
                for i in range(4):
                    mm = pe.transpose(m.ps[:, g, i * P:(i + 1) * P], keys[:, 4 * g + i], m.ident[:])
                mm.then_inc(S.keysT_full, 1)
            for n in range(LOADS):
                weights_there(pe, m, S, n)
                if n >= 2:
                    pe.wait_ge(S.used, n - 1)
                for c in range(4):
                    for k in range(KD):
                        mm = pe.matmul(m.ps[:, 4 + n % 2, c * P:(c + 1) * P], ring[n % 2][:, k, c * P:(c + 1) * P],
                                       m.hT[:, k, 0:P], start=(k == 0), stop=(k == KD - 1))
                mm.then_inc(S.full, 1)

        @block.scalar
        def _(act):
            for g in range(SUB // 4):
                act.wait_ge(S.keysT_full, g + 1)
                nc.scalar.activation(keysT[:, 4 * g:4 * g + 4], m.ps[:, g, :].rearrange("p (c n) -> p c n", n=P),
                                     ACT.Copy).then_inc(S.keysT_used, 1)

        @block.vector
        def _(dve):
            for n in range(LOADS):
                dve.wait_ge(S.full, n + 1)
                dve.tensor_copy(queries[:, 4 * n:4 * n + 4, 0:P],
                                m.ps[:, 4 + n % 2, :].rearrange("p (c n) -> p c n", n=P)).then_inc(S.used, 1)


def peer(nc, s, m, a, l):
    D, T = s.D, s.T
    UNITS, HALF = T * s.HEADS, TOPK // 2
    assert s.HEADS == 8 and HALF == SLOTS
    landed0 = 16 * 2 * UNITS * l
    queries = m.arena[:, 0:Q_WORDS].rearrange("p (c n) -> p c n", n=s.N)
    u_rows = m.arena[:, U_AT:U_AT + SLOTS * D].rearrange("p (j d) -> p j d", j=SLOTS)
    v_rows = m.arena[:, V_AT:V_AT + SLOTS * D].rearrange("p (j d) -> p j d", j=SLOTS)
    h_cur = m.arena[:, HCUR_AT:HCUR_AT + 2 * D].rearrange("p (b d) -> p b d", b=2)
    keysT = m.shift[:].rearrange("p s (c n) -> p (s c) n", n=P)
    diag = m.scale[:].rearrange("p q (j n) -> p q j n", n=P)
    w_later = m.hT[:, :, 0:P]
    CHUNKS = 2 * s.HEADS
    TWICE = CHUNKS - 4
    w_q = a.peer_w_q[l].rearrange("(k p) (c n) -> p k c n", p=P, n=P)
    free = [SEL_AT]

    def take(words):
        free[0] += words
        assert free[0] <= ARENA
        return m.arena[:, free[0] - words:free[0]]

    q_cur = take(2 * P).rearrange("p (s n) -> p s n", s=2)
    scores = take(2 * s.E).rearrange("p (s n) -> p s n", s=2)
    rest = take(2 * s.E).rearrange("p (s n) -> p s n", s=2)
    sums = take(TOPK * TOPK)
    sums_rest = take(TOPK * TOPK)
    same = take(2 * TOPK * TOPK).rearrange("p (s k j) -> p s k j", s=2, k=TOPK)
    fm = [0]

    def tiny(words, dt=F32):
        fm[0] += words
        assert fm[0] <= 256
        ap = m.small[:, fm[0] - words:fm[0]]
        return ap.bitcast(dt) if dt is not F32 else ap

    index = tiny(2 * TOPK, U32).rearrange("p (b k) -> p b k", b=2)
    gate = tiny(2 * TOPK).rearrange("p (b k) -> p b k", b=2)
    top = tiny(2 * TOPK).rearrange("p (s k) -> p s k", s=2)
    top_at = tiny(2 * TOPK, U32).rearrange("p (s k) -> p s k", s=2)
    top_atf = tiny(2 * TOPK).rearrange("p (s k) -> p s k", s=2)
    sel, sel_at = tiny(TOPK), tiny(TOPK, U32)
    ab, abf = tiny(2 * TOPK, U32).rearrange("p (s k) -> p s k", s=2), tiny(2 * TOPK).rearrange("p (s k) -> p s k", s=2)
    pair = abf
    iota = m.iota
    tail = m.tail
    neg_max, exps, exp_sum, row_f = tail[:, 0:1], tail[:, 1:17], tail[:, 17:18], tail[:, 18:34]
    dots = tail[:, 34:50].rearrange("p (q j) -> p q j", q=2)
    active = tail[:, 50:66].rearrange("p (q j) -> p q j", q=2)
    weight = tail[:, 66:82].rearrange("p (q j) -> p q j", q=2)
    u_table = a.peer_u.rearrange("l e d -> (l e) d")
    v_table = a.peer_v.rearrange("l e d -> (l e) d")
    y_banks = [m.ps[:, 2 * b:2 * b + 2, :] for b in range(2)]
    score_bank = m.ps[:, 4, 0:2 * s.E].rearrange("p (s n) -> p s n", s=2)
    later_bank = [m.ps[:, 5 + i, :] for i in range(2)]

    with phase(nc, "dotted multiplied q_staged h_staged scored scores_ready selected "
                   "index_ready best_ready exp_ready gelu_ready weight_ready diag_ready y_added y_gated chain_select "
                   "chain_first w_landed later_full later_used pool_step act_step dve_step pe_step") as (block, S):
        def every(program):
            def run(engine):
                for n in (0, 1):
                    program(engine, n, n, 1)
                with engine.Fori(2, TWICE, 2) as n:
                    program(engine, n, 0, 1)
                    program(engine, n + 1, 1, 1)
                for n in (TWICE, TWICE + 1):
                    program(engine, n, n % 2, 2)
                with engine.Fori(TWICE + 2, UNITS - 2, 2) as n:
                    program(engine, n, 0, 0)
                    program(engine, n + 1, 1, 0)
                for n in (UNITS - 2, UNITS - 1):
                    program(engine, n, n % 2, 0)
            return run

        def chunks(n, b, making):
            return [[], [(n, b)], [(2 * n - TWICE, 0), (2 * n - TWICE + 1, 1)]][making]

        def tile_head(n):
            return n // s.HEADS, n % s.HEADS

        def last(n):
            return isinstance(n, int) and n == UNITS - 1

        @block.gpsimd
        def _(pool):
            def gathers(pool, n, b, making):
                hold(pool, S.index_ready, n + 1, S.pool_step)
                for q in range(2):
                    for j in range(HALF):
                        hold(pool, S.dotted, 16 * n + 8 * q + j + 1 - SLOTS, S.pool_step)
                        at = bass.IndirectOffsetOnAxis(index[:, b, 8 * q + j:8 * q + j + 1], 0)
                        pool.indirect_dma_start(u_rows[:, j], None, u_table, at).then_inc(m.u_landed[j], 16)
                    for j in range(HALF):
                        hold(pool, S.multiplied, 16 * n + 8 * q + j + 1 - SLOTS, S.pool_step)
                        at = bass.IndirectOffsetOnAxis(index[:, b, 8 * q + j:8 * q + j + 1], 0)
                        pool.indirect_dma_start(v_rows[:, j], None, v_table, at).then_inc(m.v_landed[j], 16)

            every(gathers)(pool)

        @block.sync
        def _(sp):
            sp.dma_start(w_later, w_q[:, :, 0]).then_inc(S.w_landed, 16)
            with sp.Fori(1, CHUNKS) as c:
                sp.wait_ge(S.later_full, c)
                sp.dma_start(w_later, w_q[:, :, bass.ds(c, 1), :].rearrange("p k one n -> p k (one n)"))\
                    .then_inc(S.w_landed, 16)

        @block.scalar
        def _(act):
            def stage(n, b, queries_made=0):
                t, h = tile_head(n)
                hold(act, S.later_used, queries_made, S.act_step)
                hold(act, S.scored, n, S.act_step)
                nc.scalar.activation(q_cur, queries[:, bass.ds(2 * h, 2), bass.ds(t * P, P)], ACT.Copy)\
                    .then_inc(S.q_staged, 1)
                hold(act, S.dotted, 16 * (n - 1), S.act_step)
                nc.scalar.activation(h_cur[:, b], m.h[:, bass.ds(t, 1), :].rearrange("p one d -> p (one d)"),
                                     ACT.Copy).then_inc(S.h_staged, 1)

            def scores_out(n):
                hold(act, S.scored, n + 1, S.act_step)
                hold(act, S.selected, n, S.act_step)
                nc.scalar.activation(scores, score_bank, ACT.Copy).then_inc(S.scores_ready, 1)

            def softmax(n):
                hold(act, S.best_ready, n + 1, S.act_step)
                nc.scalar.activation(exps, sel, ACT.Exp, bias=neg_max, accum_out=exp_sum).then_inc(S.exp_ready, 1)

            def weigh(n, q):
                hold(act, S.dotted, 16 * n + 8 * q + 8, S.act_step)
                nc.scalar.activation(active[:, q], dots[:, q], ACT.Gelu).then_inc(S.gelu_ready, 1)
                hold(act, S.weight_ready, 2 * n + q + 1, S.act_step)
                hold(act, S.multiplied, 16 * (n - 1) + 8 * q + 8, S.act_step)
                for j in range(HALF):
                    nc.scalar.activation(diag[:, q, j], m.ident[:], ACT.Copy, scale=weight[:, q, j:j + 1])\
                        .then_inc(S.diag_ready, 1)

            def later_out(c, i):
                hold(act, S.later_full, c + 1, S.act_step)
                nc.scalar.activation(queries[:, bass.ds(c % CHUNKS, 1), P:s.N].rearrange("p one n -> p (one n)"),
                                     later_bank[i], ACT.Copy).then_inc(S.later_used, 1)

            def unit(act, n, b, making):
                if not last(n):
                    made = [CHUNKS, n, 2 * n - TWICE][making]
                    stage(n + 1, 1 - b, made)
                    scores_out(n + 1)
                weigh(n, 0)
                for chunk, i in chunks(n, b, making):
                    later_out(chunk, i)
                if not last(n):
                    softmax(n + 1)
                weigh(n, 1)

            stage(0, 0)
            scores_out(0)
            softmax(0)
            every(unit)(act)

        @block.tensor
        def _(pe):
            def score(n):
                _, h = tile_head(n)
                hold(pe, S.q_staged, n + 1, S.pe_step)
                hold(pe, S.scores_ready, n, S.pe_step)
                for p in range(2):
                    keys = keysT[:, bass.ds(2 * h + p, 1), :].rearrange("p one n -> p (one n)")
                    mm = pe.matmul(score_bank[:, p], q_cur[:, p], keys, start=True, stop=True)
                mm.then_inc(S.scored, 1)

            def products(n, b, q):
                if q == 0:
                    hold(pe, S.y_added, n - 1, S.pe_step)
                for j in range(HALF):
                    hold(pe, S.diag_ready, 16 * n + 8 * q + j + 1, S.pe_step)
                    hold(pe, m.v_landed[j], landed0 + 16 * (2 * n + q + 1), S.pe_step)
                    for c in range(D // 512):
                        mm = pe.matmul(y_banks[b][:, c], diag[:, q, j], v_rows[:, j, c * 512:(c + 1) * 512],
                                       start=(q == 0 and j == 0), stop=(q == 1 and j == HALF - 1))
                    mm.then_inc(S.multiplied, 1)

            def make_later(c, i):
                hold(pe, S.w_landed, 16 * (c + 1), S.pe_step)
                if not (isinstance(c, int) and c < 2):
                    hold(pe, S.later_used, c - 1, S.pe_step)
                for k in range(s.KD):
                    mm = pe.matmul(later_bank[i], w_later[:, k], m.hT[:, k, P:s.N], start=(k == 0),
                                   stop=(k == s.KD - 1))
                mm.then_inc(S.later_full, 1)

            def unit(pe, n, b, making):
                if not last(n):
                    score(n + 1)
                for chunk, i in chunks(n, b, making):
                    make_later(chunk, i)
                products(n, b, 0)
                products(n, b, 1)

            score(0)
            every(unit)(pe)

        @block.vector
        def _(dve):
            def best16(c, values, rest, best, at):
                c(dve.max(best[:, 0:8], values))
                c(dve.max_index(at[:, 0:8], best[:, 0:8], values))
                c(dve.match_replace(rest, best[:, 0:8], values, LOWEST))
                c(dve.max(best[:, 8:16], rest))
                c(dve.max_index(at[:, 8:16], best[:, 8:16], rest))

            def select_subkeys(c, n):
                hold(dve, S.scores_ready, n + 1, S.dve_step)
                for p in range(2):
                    best16(c, scores[:, p], rest[:, p], top[:, p], top_at[:, p])

            def select_experts(c, n, b):
                c(dve.tensor_copy(top_atf, top_at))
                grid = [P, TOPK, TOPK]
                c(dve.tensor_tensor(sums.rearrange("p (i j) -> p i j", i=TOPK), top[:, 0].unsqueeze(2).to_broadcast(grid),
                                    top[:, 1].unsqueeze(1).to_broadcast(grid), ALU.add))
                best16(c, sums, sums_rest, sel, sel_at)
                dve.tensor_scalar(neg_max, sel[:, 0:1], -1.0, None, ALU.mult).then_inc(S.best_ready, 1)
                c(dve.tensor_scalar(ab[:, 0], sel_at, 4, None, ALU.logical_shift_right))
                c(dve.tensor_scalar(ab[:, 1], sel_at, 15, None, ALU.bitwise_and))
                c(dve.tensor_copy(abf, ab))
                for p in range(2):
                    c(dve.tensor_tensor(same[:, p], abf[:, p].unsqueeze(2).to_broadcast(grid),
                                        iota.unsqueeze(1).to_broadcast(grid), ALU.is_equal))
                    c(dve.tensor_tensor(same[:, p], same[:, p], top_atf[:, p].unsqueeze(1).to_broadcast(grid), ALU.mult))
                c(dve.tensor_reduce(pair, same, AX.X, ALU.add))
                c(dve.tensor_scalar(row_f, pair[:, 0], float(s.E), float(l * s.E * s.E), ALU.mult, ALU.add))
                c(dve.tensor_tensor(index[:, b], row_f, pair[:, 1], ALU.add))
                dve.sem_inc(S.index_ready, 1)
                dve.sem_inc(S.selected, 1)

            PER = 3 * 5 + 2 + 3 + 2 * 2 + 3 + 2

            def meet(n, b, q):
                if q == 0:
                    hold(dve, S.h_staged, n + 1, S.dve_step)
                for j in range(HALF):
                    wait(dve, m.u_landed[j], landed0 + 16 * (2 * n + q + 1))
                    dve.tensor_tensor_reduce(u_rows[:, j], u_rows[:, j], h_cur[:, b], 1.0, 0.0, ALU.mult, ALU.add,
                                             dots[:, q, j:j + 1]).then_inc(S.dotted, 1)

            def finish_gate(c, n, b):
                hold(dve, S.exp_ready, n + 1, S.dve_step)
                c(dve.reciprocal(exp_sum, exp_sum))
                c(dve.tensor_scalar(gate[:, b], exps, exp_sum, None, ALU.mult))

            def weights(n, b, q):
                hold(dve, S.gelu_ready, 2 * n + q + 1, S.dve_step)
                dve.tensor_tensor(weight[:, q], active[:, q], gate[:, b, 8 * q:8 * q + 8], ALU.mult)\
                    .then_inc(S.weight_ready, 1)

            def add_y(n, b):
                t, _ = tile_head(n)
                row = m.x[:, bass.ds(t, 1), :].rearrange("p one d -> p (one d)")
                stream = (t + 7) // 8
                mod = m.gate[:, bass.ds(stream, 1), :].rearrange("p one d -> p (one d)")
                share = y_banks[b].rearrange("p c n -> p (c n)")
                hold(dve, S.multiplied, 16 * (n + 1), S.dve_step)
                dve.tensor_tensor(share, share, mod, ALU.mult).then_inc(S.y_gated, 1)
                hold(dve, S.y_gated, n + 1, S.dve_step)
                hold(dve, S.y_added, n, S.dve_step)
                dve.tensor_tensor(row, row, share, ALU.add).then_inc(S.y_added, 1)

            def unit(dve, n, b, making):
                c = Chain(dve, S.chain_select, PER * n, S.dve_step)
                meet(n, b, 0)
                finish_gate(c, n, b)
                weights(n, b, 0)
                if not (isinstance(n, int) and n == 0):
                    add_y(n - 1, 1 - b)
                if not last(n):
                    select_subkeys(c, n + 1)
                    select_experts(c, n + 1, 1 - b)
                    assert c.n == PER, (c.n, PER)
                meet(n, b, 1)
                weights(n, b, 1)

            first = Chain(dve, S.chain_first)
            select_subkeys(first, 0)
            select_experts(first, 0, 0)
            every(unit)(dve)
            add_y(UNITS - 1, 1)
            dve.wait_ge(S.y_added, UNITS)


def final_norm(nc, s, m, a, out):
    D, T = s.D, s.T
    gain = m.arena[:, 0:D]
    square = m.arena[:, D:2 * D]
    sumsq, rstd = m.small[:, 0:T], m.small[:, 8:8 + T]
    with phase(nc, "gain_landed chain_a std_ready chain_v y_ready stored") as (block, S):
        @block.sync
        def _(sp):
            sp.dma_start(gain, a.final_g.partition_broadcast(P)).then_inc(S.gain_landed, 16)
            sp.wait_ge(S.y_ready, 1)
            sp.dma_start(out.y_prompt, m.h[:, 0]).then_inc(S.stored, 16)
            sp.wait_ge(S.y_ready, T)
            sp.dma_start(out.y_sample.rearrange("(t p) d -> p t d", p=P), m.h[:, 1:T]).then_inc(S.stored, 16)
            sp.wait_ge(S.stored, 32)

        @block.scalar
        def _(act):
            c = Chain(act, S.chain_a)
            for t in range(T):
                c(nc.scalar.activation(square, m.x[:, t, :], ACT.Square, accum_out=sumsq[:, t:t + 1]))
            nc.scalar.activation(rstd, sumsq, ACT.Sqrt, scale=1.0 / D, bias=m.eps[:]).then_inc(S.std_ready, 1)

        @block.vector
        def _(dve):
            c = Chain(dve, S.chain_v)
            dve.wait_ge(S.std_ready, 1)
            c(dve.reciprocal(rstd, rstd))
            dve.wait_ge(S.gain_landed, 16)
            for t in range(T):
                dve.scalar_tensor_tensor(m.h[:, t, :], m.x[:, t, :], rstd[:, t:t + 1], gain, ALU.mult, ALU.mult)\
                    .then_inc(S.y_ready, 1)


QKV_AT = 8192
QT_AT = QKV_AT + 5 * 1536
CACHE_AT = QT_AT + 12 * 640


def odd_views(s, m):
    v = Memory()
    T, N = s.T, s.N
    v.hd = HEAD_DIM
    v.qkv = m.arena[:, QKV_AT:QKV_AT + T * 1536].rearrange("p (t c) -> p t c", t=T)
    v.c_qk, v.c_k, v.c_v = v.qkv[:, :, 0:640], v.qkv[:, :, 512:640], v.qkv[:, :, 640:768]
    v.d_qk, v.d_k, v.d_v = v.qkv[:, :, 768:1408], v.qkv[:, :, 1280:1408], v.qkv[:, :, 1408:1536]
    v.qT = m.arena[:, QT_AT:QT_AT + 12 * N].rearrange("p (c n) -> p c n", n=N)
    v.cache = m.arena[:, CACHE_AT:CACHE_AT + 6 * P].rearrange("p (c n) -> p c n", c=6)
    v.cacheT = m.arena[:, CACHE_AT + 6 * P:CACHE_AT + 10 * P].rearrange("p (c n) -> p c n", c=4)
    return v


def odd_slots(s, m):
    return two_slots(m, s, (0, s.KD * 512))


def odd_project(nc, s, m, a, out, j):
    KD, T = s.KD, s.T
    v = odd_views(s, m)
    w = a.odd_w_in[j]
    LOADS = w.shape[1] // 512
    assert w.shape[1] == 1536
    ring = odd_slots(s, m)
    with phase(nc, "w_landed*2 full used_scalar used_vector stored") as (block, S):
        @block.sync
        def _(sp):
            for n in range(2, LOADS):
                sp.wait_ge(S.full, T * (n - 1))
                sp.dma_start(ring[n % 2], columns(w, n)).then_inc(S.w_landed[n % 2], 16)
            sp.wait_ge(S.used_scalar, (LOADS * T + 1) // 2)
            sp.wait_ge(S.used_vector, LOADS * T // 2)
            for dst, src in ((out.cv, v.c_v), (out.dk, v.d_k), (out.dv, v.d_v)):
                sp.dma_start(dst[j].rearrange("s h d -> s (h d)"), src[:, 0]).then_inc(S.stored, 16)
            sp.wait_ge(S.stored, 48)

        @block.tensor
        def _(pe):
            for i in range(LOADS * T):
                n, t = divmod(i, T)
                if t == 0:
                    weights_there(pe, m, S, n)
                if i >= 8:
                    pe.wait_ge(S.used_scalar if i % 2 == 0 else S.used_vector, (i - 8) // 2 + 1)
                for k in range(KD):
                    mm = pe.matmul(m.ps[:, i % 8, :], m.hT[:, k, t * P:(t + 1) * P], ring[n % 2][:, k, :],
                                   start=(k == 0), stop=(k == KD - 1))
                mm.then_inc(S.full, 1)

        @block.scalar
        def _(act):
            for i in range(0, LOADS * T, 2):
                n, t = divmod(i, T)
                act.wait_ge(S.full, i + 1)
                nc.scalar.activation(v.qkv[:, t, n * 512:(n + 1) * 512], m.ps[:, i % 8, :], ACT.Copy)\
                    .then_inc(S.used_scalar, 1)

        @block.vector
        def _(dve):
            for i in range(1, LOADS * T, 2):
                n, t = divmod(i, T)
                dve.wait_ge(S.full, i + 1)
                dve.tensor_copy(v.qkv[:, t, n * 512:(n + 1) * 512], m.ps[:, i % 8, :]).then_inc(S.used_vector, 1)


def odd_heads(nc, s, m, a, out, j, l):
    T, TS = s.T, s.TS
    v = odd_views(s, m)
    hd, NH = v.hd, 640 // v.hd
    assert s.PAST == P
    squares = m.arena[:, 0:T * 640].rearrange("p (t h d) -> p t h d", t=T, d=hd)
    turned_c = m.arena[:, 3200:3200 + 4 * 320].rearrange("p (i n) -> p i n", i=4)
    turned_d = m.arena[:, 4480:4480 + 4 * 320].rearrange("p (i n) -> p i n", i=4)
    swapped = m.arena[:, 5760:5760 + T * 2 * P].rearrange("p (t c n) -> p t c n", t=T, c=2)
    gains = m.arena[:, 7040:7040 + 2 * hd].rearrange("p (g d) -> p g d", g=2)
    table = m.arena[:, 7168:7168 + TS * hd].rearrange("p (t c a f) -> p t c a f", t=TS, c=2, a=2)
    sumsq = m.small[:, 0:T * NH].rearrange("p (t h) -> p t h", t=T)
    rstd = m.small[:, 64:64 + T * NH].rearrange("p (t h) -> p t h", t=T)
    with phase(nc, ModRows.SEMS + "gains_landed table_landed cache_landed stored chain_v chain_p sum_ready "
                                  "std_ready c_normed c_ready d_ready swapped full used_scalar "
                                  "used_vector") as (block, S):
        weights = m.hT[:].rearrange("p k n -> p (k n)")[:, 0:ModRows.SLOTS * 4 * P]\
            .rearrange("p (b k n) -> p b k n", b=ModRows.SLOTS, n=P)
        spare = m.h[0:2].rearrange("p t d -> p (t d)")
        rows = ModRows(nc, s, m, a, l, 1, S, weights, spare[:, 0:3 * s.D], spare[:, 3 * s.D:3 * s.D + 512])

        @block.sync
        def _(sp):
            sp.dma_start(table, a.rope).then_inc(S.table_landed, 16)
            sp.dma_start(gains[:, 0], a.attn_qnorm_g[j].partition_broadcast(P)).then_inc(S.gains_landed, 16)
            sp.dma_start(gains[:, 1], a.attn_knorm_g[j].partition_broadcast(P)).then_inc(S.gains_landed, 16)
            for c, src in ((0, a.cache_c_k), (2, a.cache_d_k), (4, a.cache_c_v), (5, a.cache_d_v)):
                sp.dma_start(v.cache[:, c], src[0, j].rearrange("s h d -> s (h d)")).then_inc(S.cache_landed, 16)
            rows.load(sp)
            sp.wait_ge(S.c_normed, 1)
            sp.dma_start(out.ck[j].rearrange("s h d -> s (h d)"), v.c_k[:, 0]).then_inc(S.stored, 16)
            sp.wait_ge(S.cache_landed, 64)
            sp.wait_ge(S.stored, 16)

        def rotate(engine, c, qk, turned):
            for t in range(1, T):
                x = qk[:, t].rearrange("p (h a r f) -> p h a r f", h=NH, a=2, r=2)
                x1, x2 = x[:, :, :, 0], x[:, :, :, 1]
                shape = list(x1.shape)
                cos, sin = (table[:, t - 1, i].unsqueeze(1).to_broadcast(shape) for i in range(2))
                o = [turned[:, i].rearrange("p (h a f) -> p h a f", h=NH, a=2) for i in range(4)]
                for i, (part, by) in enumerate(((x1, cos), (x2, sin), (x1, sin), (x2, cos))):
                    c(engine.tensor_tensor(o[i], part, by, ALU.mult))
                c(engine.tensor_tensor(x1, o[0], o[1], ALU.subtract))
                c(engine.tensor_tensor(x2, o[2], o[3], ALU.add))

        @block.gpsimd
        def _(pool):
            c = Chain(pool, S.chain_p)
            pool.wait_ge(S.table_landed, 16)
            rotate(pool, c, v.d_qk, turned_d)
            pool.sem_inc(S.d_ready, 1)
            rows.finish(pool)

        def evacuate(g):
            src = m.ps[:, g % 8, :].rearrange("p (c n) -> p c n", n=P)
            if g == 3 * T:
                return src, v.cacheT
            t, i = divmod(g, 3)
            return src, v.qT[:, 4 * i:4 * i + 4, t * P:(t + 1) * P]

        @block.vector
        def _(dve):
            c = Chain(dve, S.chain_v)
            qk = v.c_qk.rearrange("p t (h d) -> p t h d", d=hd)
            for t in range(T):
                c(dve.tensor_tensor(squares[:, t], qk[:, t], qk[:, t], ALU.mult))
            dve.tensor_reduce(sumsq, squares, AX.X, ALU.add).then_inc(S.sum_ready, 1)
            dve.wait_ge(S.std_ready, 1)
            c(dve.reciprocal(rstd, rstd))
            dve.wait_ge(S.gains_landed, 32)
            for t in range(T):
                c(dve.tensor_tensor(qk[:, t], qk[:, t], rstd[:, t].unsqueeze(2).to_broadcast([P, NH, hd]), ALU.mult))
                for g, h0, h1 in ((0, 0, 8), (1, 8, 10)):
                    part = qk[:, t, h0:h1]
                    c(dve.tensor_tensor(part, part, gains[:, g].unsqueeze(1).to_broadcast([P, h1 - h0, hd]), ALU.mult))
            dve.sem_inc(S.c_normed, 1)
            dve.wait_ge(S.table_landed, 16)
            rotate(dve, c, v.c_qk, turned_c)
            dve.sem_inc(S.c_ready, 1)
            for g in range(1, 3 * T + 1, 2):
                dve.wait_ge(S.full, g + 1)
                src, dst = evacuate(g)
                dve.tensor_copy(dst, src).then_inc(S.used_vector, 1)

        @block.scalar
        def _(act):
            act.wait_ge(S.sum_ready, 1)
            nc.scalar.activation(rstd, sumsq, ACT.Sqrt, scale=1.0 / hd, bias=m.eps[:]).then_inc(S.std_ready, 1)
            rows.fetch(act)
            act.wait_ge(S.cache_landed, 64)
            act.wait_ge(S.c_ready, 1)
            act.wait_ge(S.d_ready, 1)
            for half in range(2):
                here, there = slice(half * hd, (half + 1) * hd), slice((1 - half) * hd, (2 - half) * hd)
                nc.scalar.activation(swapped[:, :, 0, here], v.c_k[:, :, there], ACT.Copy).then_inc(S.swapped, 1)
                nc.scalar.activation(swapped[:, :, 1, here], v.d_k[:, :, there], ACT.Copy).then_inc(S.swapped, 1)
                nc.scalar.activation(v.cache[:, 1, here], v.cache[:, 0, there], ACT.Copy).then_inc(S.swapped, 1)
                nc.scalar.activation(v.cache[:, 3, here], v.cache[:, 2, there], ACT.Copy).then_inc(S.swapped, 1)
            for g in range(0, 3 * T + 1, 2):
                act.wait_ge(S.full, g + 1)
                src, dst = evacuate(g)
                nc.scalar.activation(dst, src, ACT.Copy).then_inc(S.used_scalar, 1)

        @block.tensor
        def _(pe):
            rows.multiply(pe)
            pe.wait_ge(S.rows_fetched, rows.groups)
            pe.wait_ge(S.c_ready, 1)
            pe.wait_ge(S.d_ready, 1)
            for g in range(3 * T + 1):
                if g >= 8:
                    pe.wait_ge(S.used_scalar if g % 2 == 0 else S.used_vector, (g - 8) // 2 + 1)
                if g % 3 == 2 or g == 3 * T:
                    pe.wait_ge(S.swapped, 8)
                if g == 3 * T:
                    parts = [v.cache[:, c] for c in range(4)]
                else:
                    t, i = divmod(g, 3)
                    q = v.c_qk if i == 0 else v.d_qk
                    parts = [q[:, t, c * P:(c + 1) * P] for c in range(4)] if i < 2 else \
                        [v.c_k[:, t], swapped[:, t, 0], v.d_k[:, t], swapped[:, t, 1]]
                for c, part in enumerate(parts):
                    mm = pe.transpose(m.ps[:, g % 8, c * P:(c + 1) * P], part, m.ident[:])
                mm.then_inc(S.full, 1)


def attention(nc, s, m, a, j, early):
    T = s.T
    v = odd_views(s, m)
    hd = v.hd
    SCALE = hd ** -0.5
    GROUP = 4
    window = m.arena[:, 0:512].rearrange("p (c n) -> p c n", c=4)
    probs = m.arena[:, 512:3072].rearrange("p (b n) -> p b n", b=4)
    probsT = m.arena[:, 3072:3072 + 2 * T * GROUP * P].rearrange("p (b c h n) -> p b c h n", b=2, c=T, h=GROUP)
    assert 3072 + 2 * T * GROUP * P <= QKV_AT
    masked = m.h[:, 0, :].rearrange("p (b n) -> p b n", b=2)
    sink, neg_sink = m.small[:, 0:8], m.small[:, 8:16]
    big, neg, total, own, inv = (m.small[:, 16 + 4 * i:20 + 4 * i] for i in range(5))
    units = [(t, kind, h) for t in range(T) for kind in "CD" for h in range(8)]
    U, GROUPS = len(units), len(units) // GROUP

    def blocks(t, kind):
        if t == 0:
            return [0]
        return list(range(1, T)) + [None] if kind == "C" else \
            [b for b in (t - 1, t, t + 1) if 1 <= b < T] + [None]

    def keys(kind, h, block):
        row, kv = h % 2, h // GROUP
        c = (0 if kind == "C" else 2) + (row != kv)
        rows = slice(row * hd, (row + 1) * hd)
        return v.cacheT[rows, c] if block is None else v.qT[rows, 8 + c, block * P:(block + 1) * P]

    def values(kind, kv, block):
        cols = slice(kv * hd, (kv + 1) * hd)
        if block is None:
            return v.cache[:, 4 if kind == "C" else 5, cols]
        return (v.c_v if kind == "C" else v.d_v)[:, block, cols]

    def scores_at(i, n):
        return m.ps[:, 2 * (i % 2):2 * (i % 2) + 2, :].rearrange("p b n -> p (b n)")[:, 0:n]

    with phase(nc, "small_landed signs scores_full chain_v max_ready exp_ready inv_ready normed probsT_full probsT_used "
                   "pv_full out_ready") as (block, S):
        @block.sync
        def _(sp):
            sp.dma_start(window, a.window_masks).then_inc(S.small_landed, 16)
            sp.dma_start(sink, a.attn_sink[j].partition_broadcast(P)).then_inc(S.small_landed, 16)
            early(sp)

        @block.tensor
        def _(pe):
            def scores(i):
                t, kind, h = units[i]
                if i >= 2:
                    pe.wait_ge(S.exp_ready, i - 1)
                rows = slice(h % 2 * hd, (h % 2 + 1) * hd)
                q = v.qT[rows, (0 if kind == "C" else 4) + h // 2, t * P:(t + 1) * P]
                tiles = [b for b in blocks(t, kind) if b is not None]
                n = len(tiles) * P
                dst = scores_at(i, len(blocks(t, kind)) * P)
                span = v.qT[rows, 8 + (0 if kind == "C" else 2) + (h % 2 != h // GROUP),
                            tiles[0] * P:tiles[0] * P + n]
                mm = pe.matmul(dst[:, 0:n], q, span, start=True, stop=True)
                if t > 0:
                    mm = pe.matmul(dst[:, n:n + P], q, keys(kind, h, None), start=True, stop=True)
                mm.then_inc(S.scores_full, 1)

            def turn(i):
                t, kind, h = units[i]
                pe.wait_ge(S.normed, i + 1)
                if i >= 1:
                    pe.wait_ge(S.probsT_used, i)
                for c in range(len(blocks(t, kind))):
                    mm = pe.transpose(m.ps[:, 4 + c // 4, (c % 4) * P:(c % 4 + 1) * P],
                                      probs[:, i % 4, c * P:(c + 1) * P], m.ident[:])
                mm.then_inc(S.probsT_full, 1)

            def weigh(g, part):
                t, kind, h = units[GROUP * g]
                if part == 0:
                    pe.wait_ge(S.probsT_used, GROUP * (g + 1))
                    if g >= 2:
                        pe.wait_ge(S.out_ready, 2 * (g - 1))
                bs = blocks(t, kind)
                for c, b in enumerate(bs):
                    if min(c, GROUP - 1) != part:
                        continue
                    mm = pe.matmul(m.ps[0:hd, 6 + g % 2, :], values(kind, h // GROUP, b),
                                   probsT[:, g % 2, c].rearrange("p h n -> p (h n)"),
                                   start=(c == 0), stop=(c == len(bs) - 1))
                    if c == len(bs) - 1:
                        mm.then_inc(S.pv_full, 1)

            for i in range(U + 8):
                if i < U:
                    scores(i)
                if 0 <= i - 3 < U:
                    turn(i - 3)
                if i >= 8:
                    weigh(i // GROUP - 2, i % GROUP)

        @block.gpsimd
        def _(pool):
            for i, (t, kind, _) in enumerate(units):
                n, k = len(blocks(t, kind)) * P, i % 4
                pool.wait_ge(S.inv_ready, i + 1)
                pool.tensor_tensor(probs[:, k, 0:n], probs[:, k, 0:n], inv[:, k:k + 1].to_broadcast([P, n]),
                                   ALU.mult).then_inc(S.normed, 1)

        @block.vector
        def _(dve):
            c = Chain(dve, S.chain_v)
            dve.wait_ge(S.small_landed, 32)
            dve.tensor_scalar(neg_sink, sink, -1.0, None, ALU.mult).then_inc(S.signs, 1)
            dve.wait_ge(S.signs, 1)

            def maximum(i):
                t, kind, h = units[i]
                n, k = len(blocks(t, kind)) * P, i % 4
                dve.wait_ge(S.scores_full, i + 1)
                if i >= 2:
                    dve.wait_ge(S.exp_ready, i - 1)
                src = scores_at(i, n)
                if kind == "D" and t > 0:
                    dst = masked[:, i % 2, 0:n]
                    mask = window.rearrange("p c n -> p (c n)")
                    lo = 0 if t > 1 else P
                    local = n - P if t == T - 1 else n
                    c(dve.tensor_tensor(dst[:, 0:local], src[:, 0:local], mask[:, lo:lo + local], ALU.add))
                    if local < n:
                        c(dve.tensor_copy(dst[:, local:n], src[:, local:n]))
                    src = dst
                c(dve.reduce_max(big[:, k:k + 1], src, AX.X))
                if kind == "C":
                    dve.tensor_scalar(neg[:, k:k + 1], big[:, k:k + 1], -SCALE, None, ALU.mult)\
                        .then_inc(S.max_ready, 1)
                else:
                    dve.tensor_scalar(neg[:, k:k + 1], big[:, k:k + 1], -SCALE, neg_sink[:, h:h + 1], ALU.mult,
                                      ALU.min).then_inc(S.max_ready, 1)

            def invert(i):
                _, kind, _ = units[i]
                k = i % 4
                if i >= 4:
                    dve.wait_ge(S.normed, i - 3)
                dve.wait_ge(S.exp_ready, i + 1)
                if kind == "D":
                    c(dve.tensor_tensor(total[:, k:k + 1], total[:, k:k + 1], own[:, k:k + 1], ALU.add))
                dve.reciprocal(inv[:, k:k + 1], total[:, k:k + 1]).then_inc(S.inv_ready, 1)

            def output(g):
                t, kind, h = units[GROUP * g]
                dve.wait_ge(S.pv_full, g + 1)
                chunk = (0 if kind == "C" else 4) + h // 2
                src = m.ps[0:hd, 6 + g % 2, :].rearrange("p (c r n) -> p c r n", r=2, n=P)
                for r in range(2):
                    dve.tensor_copy(m.hT[r * hd:(r + 1) * hd, chunk:chunk + 2, t * P:(t + 1) * P], src[:, :, r])\
                        .then_inc(S.out_ready, 1)

            for i in range(U + 9):
                if i < U:
                    maximum(i)
                if 2 <= i < U + 2:
                    invert(i - 2)
                if i >= 12 and i % GROUP == 0:
                    output(i // GROUP - 3)

        @block.scalar
        def _(act):
            def exps(i):
                t, kind, h = units[i]
                n, k = len(blocks(t, kind)) * P, i % 4
                act.wait_ge(S.max_ready, i + 1)
                if i >= 4:
                    act.wait_ge(S.probsT_full, i - 3)
                src = masked[:, i % 2, 0:n] if kind == "D" and t > 0 else scores_at(i, n)
                e = nc.scalar.activation(probs[:, k, 0:n], src, ACT.Exp, scale=SCALE, bias=neg[:, k:k + 1],
                                         accum_out=total[:, k:k + 1])
                if kind == "D":
                    e = nc.scalar.activation(own[:, k:k + 1], neg[:, k:k + 1], ACT.Exp, bias=sink[:, h:h + 1])
                e.then_inc(S.exp_ready, 1)

            def evacuate(i):
                t, kind, _ = units[i]
                g, n = i // GROUP, len(blocks(t, kind))
                act.wait_ge(S.probsT_full, i + 1)
                if g >= 2 and i % GROUP == 0:
                    act.wait_ge(S.pv_full, g - 1)
                src = m.ps[:, 4:6, :].rearrange("p b n -> p (b n)").rearrange("p (c n) -> p c n", n=P)
                nc.scalar.activation(probsT[:, g % 2, 0:n, i % GROUP], src[:, 0:n], ACT.Copy)\
                    .then_inc(S.probsT_used, 1)

            for i in range(U + 4):
                if i >= 4:
                    evacuate(i - 4)
                if i < U:
                    exps(i)


GRID_W, ROPE_THETA, HEAD_DIM = 64, 10000.0, 64
INPUTS = ("x_prompt x_sample c c_ctx state_hgrn cache_c_k cache_c_v cache_d_k cache_d_v norm1_g norm2_g w_mod b_mod "
          "even_w_in even_conv_w even_w_out lb_logits hgrn_onorm_g odd_w_in attn_qnorm_g attn_knorm_g attn_sink "
          "odd_w_out peer_w_q peer_subkeys peer_u peer_v final_g").split()


def level_masks():
    import numpy as np

    s, t = np.arange(P)[:, None], np.arange(P)[None, :]
    masks = np.zeros((P, 2, LEVELS + 1, P), np.float32)
    for e in range(LEVELS):
        w = P >> (e + 1)
        same = (s // (2 * w)) == (t // (2 * w))
        masks[:, 0, e] = same & (s // w % 2 == 0) & (t // w % 2 == 1)
        masks[:, 1, e] = same & (s // w % 2 == 1) & (t // w % 2 == 0)
    masks[:, :, LEVELS] = (s == t)[:, None, :]
    return masks


def rope_table(tokens):
    import numpy as np

    f = HEAD_DIM // 4
    at = np.arange(tokens)
    inv = np.float32(ROPE_THETA) ** (-np.arange(f, dtype=np.float32) / np.float32(f))
    ang = np.stack([(at // GRID_W).astype(np.float32)[:, None] * inv, (at % GRID_W).astype(np.float32)[:, None] * inv],
                   axis=1)
    table = np.stack([np.cos(ang), np.sin(ang)], axis=1).astype(np.float32)
    return np.ascontiguousarray(table.reshape(tokens // P, P, 2, 2, f).transpose(1, 0, 2, 3, 4))


def window_masks():
    import numpy as np

    q, k = np.arange(P)[:, None], np.arange(P)[None, :]
    masks = np.zeros((P, 4, P), np.float32)
    masks[:, 0] = np.where(k >= q, 0.0, LOWEST)
    masks[:, 2] = np.where(k <= q, 0.0, LOWEST)
    return masks


def declare(nc, inputs):
    import numpy as np

    arrays = {f"in_{n}": np.ascontiguousarray(inputs[n]) for n in INPUTS}
    arrays["in_hgrn_masks"] = level_masks()
    arrays["in_rope"] = rope_table(inputs["x_sample"].shape[1])
    arrays["in_window_masks"] = window_masks()
    a = type("Inputs", (), {name[3:]: nc.dram_tensor(name, value.shape, mybir.dt.from_np(value.dtype),
                                                    kind="ExternalInput").ap() for name, value in arrays.items()})
    seq, kv = inputs["x_prompt"].shape[1], inputs["cache_c_k"].shape
    caches = (1, kv[1], seq, kv[3], kv[4])
    shapes = {"y_prompt": inputs["x_prompt"].shape, "y_sample": inputs["x_sample"].shape,
              "state": (1,) + inputs["state_hgrn"].shape[1:], "ck": caches, "cv": caches, "dk": caches, "dv": caches}
    out = type("Outputs", (), {name: nc.dram_tensor(f"out_{name}", shape, F32, kind="ExternalOutput").ap()[0]
                             for name, shape in shapes.items()})
    out.names = [f"out_{name}" for name in shapes]
    return a, out, arrays


def kernel(**inputs):
    import concourse.bacc as bacc
    from concourse.bass_utils import run_bass_kernel_spmd

    nc = bacc.Bacc("TRN2", target_bir_lowering=False, num_devices=1)
    a, out, arrays = declare(nc, inputs)
    build(nc, a, out)
    r = run_bass_kernel_spmd(nc, [arrays], core_ids=[0])
    return tuple(r.results[0][name] for name in out.names)
```
